# Optimizing a Trainium2 kernel written in Bass

```python
import math
import jax
import jax.numpy as jnp
from jax import lax
import numpy as np

D_MODEL = 1024
BATCH = 1
SEQ = 256
DEPTH = 2

N_MIXERS = 2
HEAD_DIM = 128
N_HEADS = D_MODEL // HEAD_DIM
ROPE_DIM = HEAD_DIM // 4
ROPE_THETA = 500000.0
MOBA_BLOCK = 256
MOBA_TOPK = 3
MOBA_QCHUNK = 16
HGRN_EXPAND = 128
HGRN_HEADS = D_MODEL // HGRN_EXPAND
HGRN_CHUNK = 64
D_FF = 2816
N_EXPERTS = 8
TOP_K = 2
D_FF_EXPERT = 3584
ALPHA = (2.0 * DEPTH) ** 0.25
BETA = (8.0 * DEPTH) ** -0.25
LN_EPS = 1e-5
RMS_EPS = 1e-6
N_EVEN = (DEPTH + 1) // 2
N_ODD = DEPTH // 2

kernel_name = 'hybrid_moba_hgrn2_moe_deepnorm'

def layer_norm(x, g, b):
    xf = x.astype(jnp.float32)
    mu = jnp.mean(xf, axis=-1, keepdims=True)
    var = jnp.mean(jnp.square(xf - mu), axis=-1, keepdims=True)
    return ((xf - mu) * lax.rsqrt(var + LN_EPS) * g.astype(jnp.float32) + b.astype(jnp.float32)).astype(x.dtype)

def partial_rotary(t, positions):
    half = ROPE_DIM // 2
    inv_freq = jnp.exp(-math.log(ROPE_THETA) * jnp.arange(half, dtype=jnp.float32) * (2.0 / ROPE_DIM))
    ang = positions.astype(jnp.float32)[..., None] * inv_freq
    cos = jnp.cos(ang)[:, :, None, :]
    sin = jnp.sin(ang)[:, :, None, :]
    t1 = t[..., :half].astype(jnp.float32)
    t2 = t[..., half:ROPE_DIM].astype(jnp.float32)
    rot = jnp.concatenate([t1 * cos - t2 * sin, t2 * cos + t1 * sin], axis=-1).astype(t.dtype)
    return jnp.concatenate([rot, t[..., ROPE_DIM:]], axis=-1)

def moba_attention(q, k, v):
    b_, h_, s_, hd = q.shape
    nb = -(-s_ // MOBA_BLOCK)
    pad = nb * MOBA_BLOCK - s_
    k = jnp.pad(k, ((0, 0), (0, 0), (0, pad), (0, 0)))
    v = jnp.pad(v, ((0, 0), (0, 0), (0, pad), (0, 0)))
    kb = k.reshape(b_, h_, nb, MOBA_BLOCK, hd)
    vb = v.reshape(b_, h_, nb, MOBA_BLOCK, hd)
    kmean = jnp.mean(kb.astype(jnp.float32), axis=3)
    n_top = min(MOBA_TOPK, nb)
    scale = hd ** -0.5
    take_blocks = jax.vmap(jax.vmap(lambda blocks, idx: blocks[idx]))
    blk_ids = jnp.arange(nb)
    sel_len = n_top * MOBA_BLOCK

    def chunk(ci):
        q0 = ci * MOBA_QCHUNK
        blk = q0 // MOBA_BLOCK
        qc = lax.dynamic_slice_in_dim(q, q0, MOBA_QCHUNK, axis=2).astype(jnp.float32) * scale
        qpos = q0 + jnp.arange(MOBA_QCHUNK)
        gate = jnp.einsum('bhqd,bhnd->bhqn', qc, kmean)
        gate = jnp.where(blk_ids < blk, gate, -jnp.inf)
        _, idx = lax.top_k(gate, n_top)
        valid = jnp.arange(n_top) < jnp.minimum(blk, n_top)
        k_sel = take_blocks(kb, idx)
        v_sel = take_blocks(vb, idx)
        s_sel = jnp.einsum('bhqd,bhqntd->bhqnt', qc, k_sel.astype(jnp.float32))
        s_sel = jnp.where(valid[:, None], s_sel, -jnp.inf).reshape(b_, h_, MOBA_QCHUNK, sel_len)
        k_own = lax.dynamic_slice_in_dim(k, blk * MOBA_BLOCK, MOBA_BLOCK, axis=2)
        v_own = lax.dynamic_slice_in_dim(v, blk * MOBA_BLOCK, MOBA_BLOCK, axis=2)
        kpos = blk * MOBA_BLOCK + jnp.arange(MOBA_BLOCK)
        s_own = jnp.einsum('bhqd,bhtd->bhqt', qc, k_own.astype(jnp.float32))
        s_own = jnp.where(kpos[None, :] <= qpos[:, None], s_own, -jnp.inf)
        p = jax.nn.softmax(jnp.concatenate([s_sel, s_own], axis=-1), axis=-1)
        p_sel = p[..., :sel_len].reshape(b_, h_, MOBA_QCHUNK, n_top, MOBA_BLOCK)
        p_own = p[..., sel_len:]
        o = (jnp.einsum('bhqnt,bhqntd->bhqd', p_sel, v_sel.astype(jnp.float32))
             + jnp.einsum('bhqt,bhtd->bhqd', p_own, v_own.astype(jnp.float32)))
        return o.astype(q.dtype)

    out = lax.map(chunk, jnp.arange(s_ // MOBA_QCHUNK))
    return out.transpose(1, 2, 0, 3, 4).reshape(b_, h_, s_, hd)

def moba_mixer(u, positions, w_in, w_out):
    b_, s_, d_ = u.shape
    q, k, v = jnp.split(u @ w_in, 3, axis=-1)
    heads = lambda t: t.reshape(b_, s_, N_HEADS, HEAD_DIM)
    q = partial_rotary(heads(q), positions)
    k = partial_rotary(heads(k), positions)
    v = heads(v)
    o = moba_attention(q.transpose(0, 2, 1, 3), k.transpose(0, 2, 1, 3), v.transpose(0, 2, 1, 3))
    return o.transpose(0, 2, 1, 3).reshape(b_, s_, d_) @ w_out

def hgrn2_recurrence(q, k, v, log_f):
    b_, h_, s_, dk = q.shape
    dv = v.shape[-1]
    nc = s_ // HGRN_CHUNK
    ch = lambda t: t.reshape(b_, h_, nc, HGRN_CHUNK, t.shape[-1])
    q, k, v, log_f = ch(q), ch(k), ch(v), ch(log_f)
    g_cum = jnp.cumsum(log_f, axis=3)
    q_dec = q * jnp.exp(g_cum)
    k_dec = k * jnp.exp(-g_cum)
    causal = jnp.tril(jnp.ones((HGRN_CHUNK, HGRN_CHUNK), dtype=bool))
    a = jnp.where(causal, jnp.einsum('bhncd,bhnsd->bhncs', q_dec, k_dec), 0.0)
    o_intra = jnp.einsum('bhncs,bhnsv->bhncv', a, v)
    g_last = g_cum[:, :, :, -1:, :]
    k_state = k * jnp.exp(g_last - g_cum)
    chunk_decay = jnp.exp(g_last[:, :, :, 0, :])

    def step(state, inp):
        qd, ks, vv, dec = inp
        o_inter = jnp.einsum('bhcd,bhdv->bhcv', qd, state)
        state = dec[..., None] * state + jnp.einsum('bhcd,bhcv->bhdv', ks, vv)
        return state, o_inter

    front = lambda t: t.transpose(2, 0, 1, 3, 4)
    s0 = jnp.zeros((b_, h_, dk, dv), jnp.float32)
    _, o_inter = lax.scan(step, s0, (front(q_dec), front(k_state), front(v), chunk_decay.transpose(2, 0, 1, 3)))
    o = o_intra + o_inter.transpose(1, 2, 0, 3, 4)
    return o.reshape(b_, h_, s_, dv)

def hgrn2_mixer(u, w_in, lb_logits, layer_idx, norm_w, w_out):
    b_, s_, d_ = u.shape
    q, f, i, g = jnp.split(u @ w_in, 4, axis=-1)
    sm = jax.nn.softmax(lb_logits.astype(jnp.float32), axis=0)
    lb = jnp.cumsum(sm, axis=0)[layer_idx] - sm[0]
    f_gate = lb + (1.0 - lb) * jax.nn.sigmoid(f.astype(jnp.float32))
    log_f = jnp.log(f_gate)
    key = 1.0 - f_gate
    qf = jax.nn.silu(q.astype(jnp.float32))
    heads = lambda t: t.reshape(b_, s_, HGRN_HEADS, -1).transpose(0, 2, 1, 3)
    o = hgrn2_recurrence(heads(qf), heads(key), heads(i.astype(jnp.float32)), heads(log_f))
    o = o * lax.rsqrt(jnp.mean(jnp.square(o), axis=-1, keepdims=True) + RMS_EPS)
    o = o.transpose(0, 2, 1, 3).reshape(b_, s_, d_) * norm_w.astype(jnp.float32)
    o = o * jax.nn.silu(g.astype(jnp.float32))
    return o.astype(u.dtype) @ w_out

def swiglu(u, w_gate, w_up, w_down):
    return (jax.nn.silu(u @ w_gate) * (u @ w_up)) @ w_down

def moe_swiglu(u, w_router, w_gate, w_up, w_down):
    b_, s_, d_ = u.shape
    t = u.reshape(-1, d_)
    logits = (t @ w_router).astype(jnp.float32)
    top_val, top_idx = lax.top_k(logits, TOP_K)
    top_w = jax.nn.softmax(top_val, axis=-1)
    combine = jnp.sum(jax.nn.one_hot(top_idx, N_EXPERTS, dtype=jnp.float32) * top_w[..., None], axis=1)
    y = jnp.zeros(t.shape, jnp.float32)
    for e in range(N_EXPERTS):
        y = y + combine[:, e:e + 1] * swiglu(t, w_gate[e], w_up[e], w_down[e]).astype(jnp.float32)
    return y.reshape(b_, s_, d_).astype(u.dtype)

def setup_inputs(seed: int = 0) -> dict:
    key = jax.random.key(seed)
    ks = jax.random.split(key, 24)
    d = D_MODEL
    nrm = lambda k, shape, s: jax.random.normal(k, shape, jnp.float32) * s
    x = nrm(ks[0], (BATCH, SEQ, d), 1.0)
    c = nrm(ks[1], (BATCH, d), 1.0)
    offsets = jax.random.randint(ks[2], (BATCH, 1), 0, 1024, dtype=jnp.int32)
    positions = offsets + jnp.arange(SEQ, dtype=jnp.int32)[None, :]
    ada_w = nrm(ks[3], (DEPTH, d, 6 * d), 0.1 * d ** -0.5)
    ada_b = nrm(ks[4], (DEPTH, 6 * d), 0.01)
    ln_g = 1.0 + nrm(ks[5], (DEPTH, 2, d), 0.02)
    ln_b = nrm(ks[6], (DEPTH, 2, d), 0.02)
    attn_w_in = nrm(ks[7], (N_EVEN, d, 3 * d), d ** -0.5)
    attn_w_out = nrm(ks[8], (N_EVEN, d, d), BETA * d ** -0.5)
    rec_w_in = nrm(ks[9], (N_ODD, d, 4 * d), d ** -0.5)
    rec_lb_logits = 1.0 + nrm(ks[10], (DEPTH, d), 0.1)
    rec_norm_w = 1.0 + nrm(ks[11], (N_ODD, d), 0.02)
    rec_w_out = nrm(ks[12], (N_ODD, d, d), BETA * d ** -0.5)
    ffn_w_gate = nrm(ks[13], (N_EVEN, d, D_FF), d ** -0.5)
    ffn_w_up = nrm(ks[14], (N_EVEN, d, D_FF), d ** -0.5)
    ffn_w_down = nrm(ks[15], (N_EVEN, D_FF, d), BETA * D_FF ** -0.5)
    router_w = nrm(ks[16], (N_ODD, d, N_EXPERTS), d ** -0.5)
    moe_w_gate = nrm(ks[17], (N_ODD, N_EXPERTS, d, D_FF_EXPERT), d ** -0.5)
    moe_w_up = nrm(ks[18], (N_ODD, N_EXPERTS, d, D_FF_EXPERT), d ** -0.5)
    moe_w_down = nrm(ks[19], (N_ODD, N_EXPERTS, D_FF_EXPERT, d), BETA * D_FF_EXPERT ** -0.5)
    return {'x': x, 'c': c, 'positions': positions, 'ada_w': ada_w, 'ada_b': ada_b,
            'ln_g': ln_g, 'ln_b': ln_b, 'attn_w_in': attn_w_in, 'attn_w_out': attn_w_out,
            'rec_w_in': rec_w_in, 'rec_lb_logits': rec_lb_logits, 'rec_norm_w': rec_norm_w,
            'rec_w_out': rec_w_out, 'ffn_w_gate': ffn_w_gate, 'ffn_w_up': ffn_w_up,
            'ffn_w_down': ffn_w_down, 'router_w': router_w, 'moe_w_gate': moe_w_gate,
            'moe_w_up': moe_w_up, 'moe_w_down': moe_w_down}

def reference(x, c, positions, ada_w, ada_b, ln_g, ln_b, attn_w_in, attn_w_out,
              rec_w_in, rec_lb_logits, rec_norm_w, rec_w_out, ffn_w_gate, ffn_w_up,
              ffn_w_down, router_w, moe_w_gate, moe_w_up, moe_w_down):
    mods = jnp.einsum('bd,ldm->lbm', jax.nn.silu(c), ada_w) + ada_b[:, None, :]
    for i in range(DEPTH):
        shift_m, scale_m, gate_m, shift_f, scale_f, gate_f = jnp.split(mods[i][:, None, :], 6, axis=-1)
        j = i // 2
        u = x * (1.0 + scale_m) + shift_m
        if i % N_MIXERS == 0:
            y = moba_mixer(u, positions, attn_w_in[j], attn_w_out[j])
        else:
            y = hgrn2_mixer(u, rec_w_in[j], rec_lb_logits, i, rec_norm_w[j], rec_w_out[j])
        x = layer_norm(ALPHA * x + (1.0 + gate_m) * y, ln_g[i, 0], ln_b[i, 0])
        u = x * (1.0 + scale_f) + shift_f
        if i % 2 == 0:
            y = swiglu(u, ffn_w_gate[j], ffn_w_up[j], ffn_w_down[j])
        else:
            y = moe_swiglu(u, router_w[j], moe_w_gate[j], moe_w_up[j], moe_w_down[j])
        x = layer_norm(ALPHA * x + (1.0 + gate_f) * y, ln_g[i, 1], ln_b[i, 1])
    return x


_drawn_inputs = setup_inputs


def setup_inputs(seed=0):
    import zlib

    import numpy as np

    out = dict(_drawn_inputs(seed))
    spreads = {}
    factors = {'ada_b': 3.13, 'rec_lb_logits': 7.317, 'rec_norm_w': 16.094}
    for name, (base, spread) in spreads.items():
        noise = np.random.default_rng([zlib.crc32(name.encode()), seed]).standard_normal(out[name].shape)
        drawn = base * np.exp(spread * noise) if base else spread * noise
        out[name] = jnp.asarray(drawn.astype(out[name].dtype))
    for name, factor in factors.items():
        out[name] = (out[name] * factor).astype(out[name].dtype)
    return out
```

```python
from contextlib import ExitStack

import numpy as np
import concourse.bass as bass
from concourse import mybir

ALU = mybir.AluOpType
ACT = mybir.ActivationFunctionType
AX = mybir.AxisListType
F32 = mybir.dt.float32
I32 = mybir.dt.int32
U32 = mybir.dt.uint32
U8 = mybir.dt.uint8
BF16 = mybir.dt.bfloat16

P = 128
D = 1024
SEQ = 256
NT = SEQ // P
KD = D // P
W = 512
NH = 8
HD = 128
ROPE = HD // 4
HALF = ROPE // 2
ROPE_THETA = 500000.0
CHUNK = 64
D_FF = 2816
NE = 8
D_FFE = 3584
DEPTH = 2
ALPHA = (2.0 * DEPTH) ** 0.25
LN_EPS = 1e-5
RMS_EPS = 1e-6
CAP = 128
SLOTS = 7
SCALE = HD ** -0.5
MASKED = -3.0e38

FGROUPS = [(g * W, min(W, D_FF - g * W)) for g in range(-(-D_FF // W))]
EGROUPS = D_FFE // W
ADA_UNITS = 6 * D // W
UNITS_PER_EXPERT = 3 * EGROUPS

ADA_IN_FFN = [3, 2, 2, 2, 3, 2]
ADA_STEPS = [k for n in ADA_IN_FFN for k in (n - n // 2, n // 2)]

TWO_PI = 2.0 * np.pi
PI_1 = 6.28125
PI_2 = float(np.float32(np.round((TWO_PI - PI_1) * 2.0 ** 20) / 2.0 ** 20))
PI_3 = float(np.float32(TWO_PI - PI_1 - PI_2))
ROUND = 1.5 * 2.0 ** 23
PI_F = float(np.float32(3.1415925))


def plan_stream():
    s = [("ada", j) for j in range(4)]
    s += [("qkv", 0), ("qkv", 1), ("ada", 4), ("qkv", 2), ("ada", 5), ("qkv", 3), ("ada", 6),
          ("qkv", 4), ("ada", 7), ("qkv", 5), ("ada", 8), ("ada", 9), ("wo", 0), ("wo", 1)]
    a = 10
    for g in range(len(FGROUPS)):
        s += [("gate", g), ("up", g), ("down", g)]
        s += [("ada", a + i) for i in range(ADA_IN_FFN[g])]
        a += ADA_IN_FFN[g]
    assert a == DEPTH * ADA_UNITS
    s += [("rec", n) for n in range(8)] + [("rwo", 0), ("rwo", 1)]
    return s


STREAM = plan_stream()
UNIT_AT = {u: i for i, u in enumerate(STREAM)}
MOE0 = len(STREAM)
PE_RANK, ADA_RANK = {}, {}
for _i, _u in enumerate(STREAM):
    (ADA_RANK if _u[0] == "ada" else PE_RANK)[_i] = len(ADA_RANK) if _u[0] == "ada" else len(PE_RANK)
PE_UNITS0 = len(PE_RANK)
assert all(i in PE_RANK for i in range(MOE0 - SLOTS, MOE0)) and UNITS_PER_EXPERT % SLOTS == 0


def expert_units():
    s = [("gate", 0), ("up", 0)]
    for g in range(1, EGROUPS):
        s += [("gate", g), ("up", g), ("down", g - 1)]
    return s + [("down", EGROUPS - 1)]


EXPERT_UNITS = expert_units()
EXPERT_AT = {u: i for i, u in enumerate(EXPERT_UNITS)}


def trunk_kernel(nc, x, c, positions, ada_w, ada_b, ln_g, ln_b, attn_w_in, attn_w_out, rec_w_in,
                 rec_lb_logits, rec_norm_w, rec_w_out, ffn_w_gate, ffn_w_up, ffn_w_down, router_w,
                 moe_w_gate, moe_w_up, moe_w_down, out):
    with ExitStack() as ctx:
        def sb(name, shape, dt=F32):
            return ctx.enter_context(nc.sbuf_tensor(name, shape, dt))

        def sem(name):
            return ctx.enter_context(nc.semaphore(name))

        ring = sb("ring", [P, SLOTS, 4096])
        u_f = sb("u_f", [P, KD, SEQ])
        big_a = sb("big_a", [P, KD, SEQ])
        arena = sb("arena", [P, 3, KD * SEQ])
        tok = sb("tok", [P, NT, 3 * D])
        x_t = sb("x_t", [P, NT, D])
        y_t = sb("y_t", [P, NT, D])
        h_t = sb("h_t", [P, W])
        h_f = sb("h_f", [P, 4, P])
        acc = sb("acc", [P, 2, W])
        ident = sb("ident", [P, P])
        ones = sb("ones", [P, P])
        before = sb("before", [P, P])
        future = sb("future", [P, P], U8)
        keep = sb("keep", [P, NT, P], U8)
        neg = sb("neg", [P, 1])
        carry = sb("carry", [P, SEQ], BF16)
        iota = sb("iota", [P, 2 * CAP], BF16)
        adab = sb("adab", [DEPTH * ADA_UNITS, W])
        ccol = sb("ccol", [P, KD])
        modc = sb("modc", [P, DEPTH, 6 * KD])
        invf = sb("invf", [P, HALF])
        pos_i = sb("pos_i", [P, NT], I32)
        pos_f = sb("pos_f", [P, NT])
        ang = sb("ang", [P, 4, NT, HALF])
        lbc = sb("lbc", [P, 8, KD])
        normc = sb("normc", [P, KD])
        stat = sb("stat", [P, NT, 16])
        sm = sb("sm", [P, 2, 8])
        last = sb("last", [P, 2, NH, 4])
        rms = sb("rms", [P, NT, 2, NH])
        wr = sb("wr", [P, KD, NE])
        rt = sb("rt", [P, NT, 8, NE])
        ridx = sb("ridx", [P, NT, 8], U32)
        over = sb("over", [P, 2])
        flag = sb("flag", [P, 1], I32)
        c_rows = h_t[0:KD, 0:P]
        lb_rows = h_t[0:DEPTH * KD, P:2 * P]
        nw_rows = h_t[0:KD, 2 * P:3 * P]

        bank = [ctx.enter_context(nc.psum_tensor(f"bank{i}", [P, W], F32)) for i in range(8)]
        PAIR = bank[0:2]
        GATE_B, UP_B, TURN_B, SMALL_B = bank[0:4]
        Y_B = bank[4:8]

        buf_b, buf_c, buf_d = (arena[:, i, :].rearrange("p (k s) -> p k s", k=KD) for i in range(3))
        q_f, k_f, o_f = big_a, buf_b, buf_c
        flat_d = arena[:, 2, :]
        probs = flat_d[:, 0:768].rearrange("p (b n) -> p b n", b=2)
        probs_f = flat_d[:, 768:1536].rearrange("p (b n) -> p b n", b=2)
        v_t = tok[:, :, 2 * D:3 * D]
        gate_row = tok[:, 0, D:2 * D]
        g_row = tok[:, 0, 0:D]
        b_row = tok[:, 1, 0:D]
        flat_all = arena[:, :, :].rearrange("p a n -> p (a n)")
        pick = flat_all[:, 0:(NE + 1) * SEQ]
        put_all = flat_all[:, (NE + 1) * SEQ:(2 * NE + 2) * SEQ]
        ye = flat_all[:, (2 * NE + 2) * SEQ:(2 * NE + 2) * SEQ + D]
        put = flat_all[:, (2 * NE + 2) * SEQ + D:(2 * NE + 3) * SEQ + D]
        put_raw = u_f[:, :, :].rearrange("p k s -> p (k s)")
        ks_t = put_raw.rearrange("p (t d) -> p t d", t=NT)
        intra = flat_d[:, 0:2 * SEQ].rearrange("p (b s) -> p b s", b=2)
        states = flat_d[:, 2 * SEQ:2 * SEQ + 6 * HD].rearrange("p (b j n) -> p b j n", b=2, j=3)
        y_flat = y_t[:, :, :].rearrange("p t d -> p (t d)")
        diags = [y_flat[:, 0:D], flat_d[:, 0:D], y_flat[:, 0:D],
                 big_a[:, :, :].rearrange("p k s -> p (k s)")[:, D:2 * D]]
        kv_products = [TURN_B[:, 0:P], SMALL_B[:, 0:P], TURN_B[:, P:2 * P]]
        ue_f = big_a[:, :, :].rearrange("p k s -> p (k s)").rearrange("p (b k s) -> p b k s", b=2, k=KD)

        slot_filled = [sem(f"slot_filled{i}") for i in range(SLOTS)]
        x_loaded = sem("x_loaded")
        smalls_loaded = sem("smalls_loaded")
        consts_ready = sem("consts_ready")
        pool_step = sem("pool_step")
        dve_step = sem("dve_step")
        rows_turned = sem("rows_turned")
        c_ready = sem("c_ready")
        lb_logits_ready = sem("lb_logits_ready")
        lb_exp_ready = sem("lb_exp_ready")
        angles_ready = sem("angles_ready")
        sincos_ready = sem("sincos_ready")
        ada_summed = sem("ada_summed")
        ada_cols_full = sem("ada_cols_full")
        ada_cols_read = sem("ada_cols_read")
        pair_full = sem("pair_full")
        pair_free = sem("pair_free")
        rotated = sem("rotated")
        row_max_ready = sem("row_max_ready")
        probs_ready = sem("probs_ready")
        turn_full = sem("turn_full")
        turn_free = sem("turn_free")
        head_full = sem("head_full")
        head_free = sem("head_free")
        y_full = sem("y_full")
        y_read = sem("y_read")
        diag_ready = sem("diag_ready")
        var_ready = sem("var_ready")
        std_ready = sem("std_ready")
        x_ready = sem("x_ready")
        ln_rows = sem("ln_rows")
        gate_full = sem("gate_full")
        silu_ready = sem("silu_ready")
        up_full = sem("up_full")
        h_ready = sem("h_ready")
        hturn_full = sem("hturn_full")
        hf_ready = sem("hf_ready")
        recturn_full = sem("recturn_full")
        recturn_read = sem("recturn_read")
        rows_read = sem("rows_read")
        down_done = sem("down_done")
        fgate_ready = sem("fgate_ready")
        logf_ready = sem("logf_ready")
        gcum_ready = sem("gcum_ready")
        expg_ready = sem("expg_ready")
        expg_used = sem("expg_used")
        expng_ready = sem("expng_ready")
        expst_ready = sem("expst_ready")
        decs_ready = sem("decs_ready")
        kv_full = sem("kv_full")
        states_ready = sem("states_ready")
        o_full = sem("o_full")
        o_ready = sem("o_ready")
        sq_ready = sem("sq_ready")
        msq_ready = sem("msq_ready")
        rms_ready = sem("rms_ready")
        o_gated = sem("o_gated")
        logits_full = sem("logits_full")
        gap_ready = sem("gap_ready")
        gap_exp = sem("gap_exp")
        masks_ready = sem("masks_ready")
        places_full = sem("places_full")
        flag_ready = sem("flag_ready")
        out_stored = sem("out_stored")
        moe_sems = [{k: sem(f"{k}_{p}") for k in (
            "picks_ready", "pick_full", "ue_ready", "gate_full", "silu_ready", "up_full", "h_ready",
            "hturn_full", "hf_ready", "down_done", "ye_ready", "put_ready", "put_full", "put_added")} for p in range(2)]

        def wide(s):
            return ring[:, s, :].rearrange("p (k n) -> p k n", n=W)

        def tall(s):
            return ring[:, s, :].rearrange("p (k n) -> p k n", n=D)

        def columns(w, lo, n):
            return w.rearrange("(k p) n -> p k n", p=P)[:, :, lo:lo + n]

        def prologue_source(kind, a):
            if kind == "ada":
                return wide, W, columns(ada_w[a // ADA_UNITS], a % ADA_UNITS * W, W)
            if kind in ("qkv", "wo", "rec", "rwo"):
                w = {"qkv": attn_w_in, "wo": attn_w_out, "rec": rec_w_in, "rwo": rec_w_out}[kind]
                return wide, W, columns(w[0], a * W, W)
            lo, n = FGROUPS[a]
            if kind == "down":
                return tall, n // P, ffn_w_down[0, lo:lo + n, :].rearrange("(k p) n -> p k n", p=P)
            return wide, n, columns((ffn_w_gate if kind == "gate" else ffn_w_up)[0], lo, n)

        block = ctx.enter_context(nc.Block())

        def arrived(eng, i):
            eng.wait_ge(slot_filled[i % SLOTS], 16 * (i // SLOTS + 1))
            return i % SLOTS

        PAIR_AT, n = {}, 0
        for stage, count in (("mod0", 4), ("qk", 8), ("v0", 2), ("turn_q", 4), ("v1", 2), ("turn_k", 4),
                             ("gate_row0", 2), ("scores", NH), ("mod1", 4), ("gate_row1", 2), ("mod2", 4),
                             ("rec", 16), ("turn_ks", 4), ("intra", NH), ("turn_o", 4), ("gate_row2", 2),
                             ("mod3", 4), ("gate_row3", 2), ("turn_put", 4), ("turn_put2", 4), ("end", 0)):
            PAIR_AT[stage], n = n, n + count

        def pair_claim(pe, n):
            if n >= 2:
                pe.wait_ge(pair_free, n - 1)
            return PAIR[n % 2]

        def used(i):
            kind, a = STREAM[i]
            if kind == "ada":
                return ada_summed, a + 1
            if kind == "qkv":
                first = {4: PAIR_AT["v0"], 5: PAIR_AT["v1"]}.get(a, PAIR_AT["qk"] + NT * a)
                return pair_full, first + NT
            if kind == "rec":
                return pair_full, PAIR_AT["rec"] + NT * (a + 1)
            if kind in ("wo", "rwo"):
                return y_full, (4 if kind == "rwo" else 0) + NT * (a + 1)
            return {"gate": gate_full, "up": up_full, "down": down_done}[kind], NT * (a + 1)

        EXPERT_DONE = {"gate": "gate_full", "up": "up_full", "down": "down_done"}

        @block.sync
        def _(sp):
            for i, (kind, a) in enumerate(STREAM):
                if i >= SLOTS:
                    sp.wait_ge(*used(i - SLOTS))
                view, n, src = prologue_source(kind, a)
                dst = view(i % SLOTS)
                dst = dst[:, 0:n, :] if kind == "down" else dst[:, :, 0:n]
                sp.dma_start(dst, src).then_inc(slot_filled[i % SLOTS], 16)

            def load_expert_unit(e, i):
                kind, g = EXPERT_UNITS[i]
                s = (MOE0 + i) % SLOTS
                if kind == "down":
                    w = moe_w_down[0].rearrange("e (k p) n -> p e k n", p=P)
                    src = w[:, bass.ds(e, 1), 4 * g:4 * g + 4, :]
                    dst = tall(s)
                else:
                    w = (moe_w_gate if kind == "gate" else moe_w_up)[0].rearrange("e (k p) n -> p e k n", p=P)
                    src = w[:, bass.ds(e, 1), :, g * W:(g + 1) * W]
                    dst = wide(s)
                sp.dma_start(dst, src.rearrange("p e k n -> p (e k) n")).then_inc(slot_filled[s], 16)

            def wait_expert_unit_used(me, e, i):
                kind, g = EXPERT_UNITS[i]
                sp.wait_ge(me[EXPERT_DONE[kind]], e * EGROUPS + (g + 1))

            def expert_weights(p):
                me = moe_sems[p]
                for i in range(SLOTS):
                    if p == 0:
                        sp.wait_ge(*used(MOE0 + i - SLOTS))
                    else:
                        wait_expert_unit_used(moe_sems[0], NE - 1, UNITS_PER_EXPERT - SLOTS + i)
                    load_expert_unit(0, i)
                with sp.Fori(0, NE - 1) as e:
                    for i in range(SLOTS, UNITS_PER_EXPERT):
                        wait_expert_unit_used(me, e, i - SLOTS)
                        load_expert_unit(e, i)
                    for i in range(SLOTS):
                        wait_expert_unit_used(me, e, UNITS_PER_EXPERT - SLOTS + i)
                        load_expert_unit(e + 1, i)
                for i in range(SLOTS, UNITS_PER_EXPERT):
                    wait_expert_unit_used(me, NE - 1, i - SLOTS)
                    load_expert_unit(NE - 1, i)

            expert_weights(0)
            sp.wait_ge(flag_ready, 1)
            overflow = sp.value_load(flag[0:1, 0:1], min_val=0, max_val=1)
            with sp.If(overflow > 0):
                expert_weights(1)

        @block.gpsimd
        def _(pool):
            n = [0]

            def step(ins):
                n[0] += 1
                ins.then_inc(pool_step, 1)

            def settled():
                pool.wait_ge(pool_step, n[0])

            step(pool.memset(ident[:], 0.0))
            step(pool.memset(ones[:], 1.0))
            step(pool.memset(neg[:], MASKED))
            step(pool.memset(carry[:], 1.0))
            f = np.exp(np.float32(-np.log(ROPE_THETA)) * np.arange(HALF, dtype=np.float32) * np.float32(2.0 / ROPE))
            for j in range(HALF):
                step(pool.memset(invf[:, j:j + 1], float(np.float32(f[j]))))
            step(pool.iota(iota[:], pattern=[[1, 2 * CAP]], base=0, channel_multiplier=0,
                           allow_small_or_imprecise_dtypes=True))
            settled()
            step(pool.affine_select(out=ident[:], in_=ident[:], compare_op=ALU.not_equal, fill=1.0,
                                    base=0, pattern=[[-1, P]], channel_multiplier=1))
            step(pool.affine_select(out=before[:], in_=ones[:], compare_op=ALU.is_gt, fill=0.0,
                                    base=0, pattern=[[1, P]], channel_multiplier=-1))
            step(pool.memset(carry[:].rearrange("p (c s) -> p c s", s=CHUNK)[:, :, 0:1], 0.0))
            settled()
            step(pool.tensor_copy(future[:], before[:]))
            diag = h_f[:, 0:NT, :]
            step(pool.affine_select(out=diag, in_=ones[:].unsqueeze(1).to_broadcast([P, NT, P]),
                                    compare_op=ALU.is_ge, fill=0.0,
                                    base=0, pattern=[[0, NT], [1, P]], channel_multiplier=-1))
            settled()
            for t in range(NT):
                step(pool.memset(h_f[0:CHUNK, t, CHUNK:P], 0.0))
            settled()
            step(pool.tensor_copy(keep[:], diag))
            settled()
            pool.memset(acc[:, 0, 0:1], 0.0).then_inc(consts_ready, 1)

        @block.scalar
        def _(act):
            pair = [0]

            def pair_take():
                act.wait_ge(pair_full, pair[0] + 1)
                pair[0] += 1
                return PAIR[(pair[0] - 1) % 2]

            act.dma_start(h_t[0:KD, 0:P], c.rearrange("b (k p) -> (b k) p", p=P)).then_inc(smalls_loaded, 16)
            act.dma_start(x_t[:], x[0].rearrange("(t p) d -> p t d", p=P)).then_inc(x_loaded, 16)
            act.dma_start(adab[:], ada_b.rearrange("l (j w) -> (l j) w", w=W)).then_inc(smalls_loaded, 16)
            act.dma_start(lb_rows, rec_lb_logits.rearrange("l (k p) -> (l k) p", p=P)).then_inc(smalls_loaded, 16)
            act.dma_start(nw_rows, rec_norm_w.rearrange("l (k p) -> (l k) p", p=P)).then_inc(smalls_loaded, 16)
            with nc.allow_non_contiguous_dma(reason="256 positions, one per partition and tile"):
                act.dma_start(pos_i[:], positions.rearrange("b (t p) -> p (b t)", p=P)).then_inc(smalls_loaded, 16)
            act.dma_start(wr[:], router_w[0].rearrange("(k p) e -> p k e", p=P)).then_inc(smalls_loaded, 16)

            act.wait_ge(rows_turned, 1)
            act.activation(ccol[:], SMALL_B[:, 0:KD], ACT.Silu).then_inc(c_ready, 1)
            def modulate(layer, vec):
                act.wait_ge(ada_cols_read, ADA_UNITS * layer + 2 * (vec + 2))
                for t in range(NT):
                    for half in range(2):
                        b = pair_take()
                        for j in range(4):
                            k = 4 * half + j
                            ins = act.activation(u_f[:, k, t * P:(t + 1) * P], b[:, j * P:(j + 1) * P], ACT.Identity,
                                                 scale=modc[:, layer, (vec + 1) * KD + k:(vec + 1) * KD + k + 1],
                                                 bias=modc[:, layer, vec * KD + k:vec * KD + k + 1])
                        ins.then_inc(pair_free, 1)

            def empty(dst, func=ACT.Copy, **kw):
                b = pair_take()
                act.activation(dst, b[:, 0:dst.free_size()], func, **kw).then_inc(pair_free, 1)

            def take_gate_row():
                for half in range(2):
                    empty(gate_row[:, half * W:(half + 1) * W])

            def load_ln_rows(layer, sub):
                act.dma_start(g_row, ln_g[layer, sub, :].partition_broadcast(P)).then_inc(ln_rows, 16)
                act.dma_start(b_row, ln_b[layer, sub, :].partition_broadcast(P)).then_inc(ln_rows, 16)

            def deviations(stage):
                for t in range(NT):
                    act.wait_ge(var_ready, NT * stage + t + 1)
                    act.activation(stat[:, t, 14:15], stat[:, t, 13:14], ACT.Sqrt).then_inc(std_ready, 1)

            modulate(0, 0)
            act.wait_ge(angles_ready, 1)
            act.activation(ang[:, 2:4], ang[:, 2:4], ACT.Sin).then_inc(sincos_ready, 1)
            act.wait_ge(lb_logits_ready, 1)
            act.activation(lbc[:, 3:5, :], lbc[:, 0:2, :], ACT.Exp).then_inc(lb_exp_ready, 1)
            for u in range(4):
                for t in range(NT):
                    empty(tok[:, t, u * W:(u + 1) * W])
            for t in range(NT):
                empty(tok[:, t, 4 * W:5 * W])
            for j in range(4):
                empty(q_f[:, 2 * j:2 * j + 2, :].rearrange("p k s -> p (k s)"))
            load_ln_rows(0, 0)
            for t in range(NT):
                empty(tok[:, t, 5 * W:6 * W])
            for j in range(4):
                empty(k_f[:, 2 * j:2 * j + 2, :].rearrange("p k s -> p (k s)"))
            take_gate_row()

            for h in range(NH + 2):
                if h < NH:
                    b = pair_take()
                    r = h % 2
                    act.wait_ge(row_max_ready, h + 1)
                    if h >= 2:
                        act.wait_ge(turn_full, h - 1)
                    act.activation(probs[:, r, 0:P], b[:, 0:P], ACT.Exp, bias=sm[:, r, 2:3], scale=SCALE,
                                   accum_out=sm[:, r, 4:5])
                    act.activation(probs[:, r, P:3 * P], b[:, P:3 * P], ACT.Exp, bias=sm[:, r, 3:4], scale=SCALE,
                                         accum_out=sm[:, r, 5:6]).then_inc(pair_free, 1)
                if 1 <= h <= NH:
                    act.wait_ge(turn_full, h)
                    if h >= 3:
                        act.wait_ge(head_full, h - 2)
                    act.activation(probs_f[:, (h - 1) % 2, :], TURN_B[:, 0:3 * P], ACT.Copy).then_inc(turn_free, 1)
                if h >= 2:
                    act.wait_ge(head_full, h - 1)
                    act.activation(o_f[:, h - 2, :], Y_B[0][:, 0:SEQ], ACT.Copy).then_inc(head_free, 1)
            deviations(0)
            modulate(0, 3)

            act.wait_ge(x_ready, NT)
            load_ln_rows(0, 1)

            FSTEPS = len(FGROUPS) * NT
            for s in range(FSTEPS + 1):
                if s < FSTEPS:
                    width = FGROUPS[s // NT][1]
                    act.wait_ge(gate_full, s + 1)
                    if s >= 1:
                        act.wait_ge(hturn_full, s)
                    act.activation(h_t[:, 0:width], GATE_B[:, 0:width], ACT.Silu).then_inc(silu_ready, 1)
                if s >= 1:
                    width = FGROUPS[(s - 1) // NT][1]
                    act.wait_ge(hturn_full, s)
                    act.activation(h_f[:, 0:width // P, :].rearrange("p k s -> p (k s)"), TURN_B[:, 0:width],
                                   ACT.Copy).then_inc(hf_ready, 1)
            take_gate_row()
            deviations(1)
            modulate(1, 0)

            for u in range(8):
                for t in range(NT):
                    i = NT * u + t
                    if u < 4:
                        if i >= 2:
                            act.wait_ge(recturn_full, i - 1)
                        dst = h_t[:] if i % 2 == 0 else h_f[:].rearrange("p k s -> p (k s)")
                        empty(dst, ACT.Silu if u < 2 else ACT.Sigmoid)
                    elif u < 6:
                        empty(v_t[:, t, (u - 4) * W:(u - 3) * W])
                    else:
                        empty(y_t[:, t, (u - 6) * W:(u - 5) * W], ACT.Silu)
            act.wait_ge(fgate_ready, 1)
            act.activation(buf_c[:], buf_c[:], ACT.Ln).then_inc(logf_ready, 1)
            act.wait_ge(gcum_ready, 1)
            act.activation(last[:, 1], last[:, 0], ACT.Exp).then_inc(expg_ready, 1)
            act.activation(buf_c[:], buf_d[:], ACT.Exp).then_inc(expg_ready, 1)
            act.wait_ge(expg_used, 1)
            act.activation(buf_c[:], buf_d[:], ACT.Exp, scale=-1.0).then_inc(expng_ready, 1)
            act.wait_ge(expng_ready, 1)
            for h in range(NH):
                for j in range(3):
                    cols = buf_d[:, h, j * CHUNK:(j + 1) * CHUNK]
                    act.activation(cols, cols, ACT.Exp, bias=last[:, 0, h, j:j + 1], scale=-1.0).then_inc(expst_ready, 1)
            for j in range(4):
                t, half = j // 2, j % 2
                empty(u_f[:].rearrange("p k s -> p (k s)")[:, t * D + half * W:t * D + (half + 1) * W])
            for h in range(NH):
                pair[0] += 1
                if h % 4 == 3:
                    for t in range(NT):
                        act.wait_ge(o_full, NT * h + t + 1)
                        sl = slice(h // 4 * W, (h // 4 + 1) * W)
                        act.activation(tok[:, t, sl], Y_B[2 * t + h // 4][:], ACT.Copy).then_inc(o_ready, 1)
            for t in range(NT):
                for half in range(2):
                    act.activation(tok[:, t, D + half * W:D + (half + 1) * W], Y_B[2 * t + half][:],
                                   ACT.Square).then_inc(sq_ready, 1)
            for t in range(NT):
                act.wait_ge(msq_ready, t + 1)
                act.activation(rms[:, t, 1, :], rms[:, t, 0, :], ACT.Sqrt).then_inc(rms_ready, 1)
            for t in range(NT):
                for half in range(2):
                    b = pair_take()
                    for j in range(4):
                        k = 4 * half + j
                        ins = act.activation(o_f[:, k, t * P:(t + 1) * P], b[:, j * P:(j + 1) * P], ACT.Copy,
                                             scale=normc[:, k:k + 1])
                    ins.then_inc(pair_free, 1)
            load_ln_rows(1, 0)
            take_gate_row()
            deviations(2)
            modulate(1, 3)

            act.wait_ge(x_ready, 3 * NT)
            load_ln_rows(1, 1)
            for t in range(NT):
                act.wait_ge(gap_ready, t + 1)
                act.activation(rt[:, t, 5, 2:3], rt[:, t, 5, 0:1], ACT.Exp).then_inc(gap_exp, 1)

            take_gate_row()

            def experts(p):
                me = moe_sems[p]

                def gathered(count, half, buffer):
                    act.wait_ge(me["pick_full"], count)
                    for j in range(4):
                        k = 4 * half + j
                        ins = act.activation(ue_f[:, buffer, k, :], SMALL_B[:, j * P:(j + 1) * P], ACT.Identity,
                                             scale=modc[:, 1, 4 * KD + k:4 * KD + k + 1],
                                             bias=modc[:, 1, 3 * KD + k:3 * KD + k + 1])
                    ins.then_inc(me["ue_ready"], 1)

                def turned(count):
                    act.wait_ge(me["hturn_full"], count)
                    act.activation(h_f[:].rearrange("p k s -> p (k s)"), TURN_B[:], ACT.Copy)\
                       .then_inc(me["hf_ready"], 1)

                for j in range(4):
                    empty(put_all[:, SEQ + j * W:SEQ + (j + 1) * W])
                for half in range(2):
                    gathered(half + 1, half, 0)
                act.sem_inc(me["ye_ready"], 1)
                with act.Fori(0, NE // 2) as pr:
                    for r in range(2):
                        for g in range(EGROUPS):
                            done = pr * (2 * EGROUPS) + (r * EGROUPS + g)
                            act.wait_ge(me["gate_full"], done + 1)
                            if g >= 1:
                                act.wait_ge(me["hturn_full"], done)
                            act.activation(h_t[:], GATE_B[:], ACT.Silu).then_inc(me["silu_ready"], 1)
                            if g >= 1:
                                turned(done)
                            if g in (2, 4):
                                half = g // 2 - 1
                                gathered(pr * 4 + (2 * r + 2 + half + 1), half, (r + 1) % 2)
                        turned(pr * (2 * EGROUPS) + (r + 1) * EGROUPS)
                        act.wait_ge(me["down_done"], pr * (2 * EGROUPS) + (r + 1) * EGROUPS)
                        for half in range(2):
                            act.activation(ye[:, half * W:(half + 1) * W], Y_B[half][:],
                                           ACT.Copy).then_inc(me["ye_ready"], 1)

            experts(0)
            act.wait_ge(flag_ready, 1)
            overflow = act.value_load(flag[0:1, 0:1], min_val=0, max_val=1)
            with act.If(overflow > 0):
                experts(1)
            deviations(3)
            for t in range(NT):
                act.wait_ge(x_ready, 3 * NT + t + 1)
                act.dma_start(out[0, t * P:(t + 1) * P, :], x_t[:, t, :]).then_inc(out_stored, 16)
            act.wait_ge(out_stored, 16 * NT)

        @block.tensor
        def _(pe):
            pair = [0]

            def claim():
                n, pair[0] = pair[0], pair[0] + 1
                return pair_claim(pe, n)

            def product(dst, lhs_f, t, slot, n=W):
                for k in range(KD):
                    ins = pe.matmul(dst[:, 0:n], lhs_f[:, k, t * P:(t + 1) * P], wide(slot)[:, k, 0:n],
                                    start=(k == 0), stop=(k == KD - 1))
                return ins

            def turn_four(dst, ins_of):
                for j in range(4):
                    ins = pe.transpose(dst[:, j * P:(j + 1) * P], ins_of(j), ident[:])
                return ins

            def add_partitions(a):
                if a:
                    pe.wait_ge(ada_cols_read, a)
                pe.wait_ge(ada_summed, a + 1)
                for j in range(4):
                    pe.matmul(SMALL_B[:, j:j + 1], acc[:, a % 2, j * P:(j + 1) * P], ones[:, 0:1], start=True, stop=False)
                    ins = pe.matmul(SMALL_B[:, j:j + 1], adab[:, j * P:(j + 1) * P],
                                    ident[0:DEPTH * ADA_UNITS, a:a + 1], start=False, stop=True)
                ins.then_inc(ada_cols_full, 1)

            def turn_x(stage, tiles=range(NT)):
                for t in tiles:
                    if stage:
                        pe.wait_ge(x_ready, NT * (stage - 1) + t + 1)
                    for half in range(2):
                        turn_four(claim(), lambda j: x_t[:, t, (4 * half + j) * P:(4 * half + j + 1) * P])\
                            .then_inc(pair_full, 1)

            def gate_row_product(stage):
                pe.wait_ge(diag_ready, stage + 1)
                for half in range(2):
                    pe.matmul(claim()[:], ones[:], diags[stage][:, half * W:(half + 1) * W],
                              start=True, stop=True).then_inc(pair_full, 1)

            pe.wait_ge(consts_ready, 1)
            pe.wait_ge(smalls_loaded, 16 * 6)
            pe.transpose(SMALL_B[:, 0:KD], c_rows, ident[0:KD, 0:KD])
            pe.transpose(SMALL_B[:, KD:3 * KD], lb_rows, ident[0:2 * KD, 0:2 * KD])
            pe.transpose(SMALL_B[:, 3 * KD:4 * KD], nw_rows, ident[0:KD, 0:KD]).then_inc(rows_turned, 1)
            pe.wait_ge(x_loaded, 16)
            turn_x(0, [0])
            pe.wait_ge(c_ready, 1)
            pe.wait_ge(rows_read, 1)
            for a in range(4):
                add_partitions(a)
            turn_x(0, [1])

            def project_qkv(u):
                s = arrived(pe, UNIT_AT["qkv", u])
                for t in range(NT):
                    product(claim(), u_f, t, s).then_inc(pair_full, 1)

            pe.wait_ge(pair_free, PAIR_AT["qk"])
            project_qkv(0)
            project_qkv(1)
            add_partitions(4)
            project_qkv(2)
            add_partitions(5)
            project_qkv(3)
            add_partitions(6)
            project_qkv(4)
            pe.wait_ge(rotated, NT)

            def turn_heads(first_column):
                for j in range(4):
                    turn_four(claim(), lambda i: tok[:, i % 2, first_column + (2 * j + i // 2) * P:
                                                     first_column + (2 * j + i // 2 + 1) * P]).then_inc(pair_full, 1)

            turn_heads(0)
            project_qkv(5)
            turn_heads(D)
            for a in (7, 8, 9):
                add_partitions(a)
            gate_row_product(0)
            pe.wait_ge(pair_free, PAIR_AT["gate_row0"])
            for i in range(NH + 2):
                if i < NH:
                    b = claim()
                    pe.matmul(b[:, 0:P], q_f[:, i, 0:P], k_f[:, i, 0:P], start=True, stop=True)
                    pe.matmul(b[:, P:3 * P], q_f[:, i, P:SEQ], k_f[:, i, :], start=True, stop=True).then_inc(pair_full, 1)
                if 1 <= i <= NH:
                    h = i - 1
                    pe.wait_ge(probs_ready, h + 1)
                    if h:
                        pe.wait_ge(turn_free, h)
                    for j in range(3):
                        ins = pe.transpose(TURN_B[:, j * P:(j + 1) * P], probs[:, h % 2, j * P:(j + 1) * P], ident[:])
                    ins.then_inc(turn_full, 1)
                if i >= 2:
                    h = i - 2
                    pe.wait_ge(turn_free, h + 1)
                    if h:
                        pe.wait_ge(head_free, h)
                    pe.matmul(Y_B[0][:, 0:SEQ], v_t[:, 0, h * P:(h + 1) * P], probs_f[:, h % 2, 0:SEQ],
                              start=True, stop=False)
                    pe.matmul(Y_B[0][:, P:SEQ], v_t[:, 1, h * P:(h + 1) * P], probs_f[:, h % 2, SEQ:SEQ + P],
                              start=False, stop=True).then_inc(head_full, 1)
            pe.wait_ge(head_free, NH)
            for u in range(2):
                s = arrived(pe, UNIT_AT["wo", u])
                for t in range(NT):
                    product(Y_B[2 * t + u], o_f, t, s).then_inc(y_full, 1)
            turn_x(1)

            pe.wait_ge(pair_free, PAIR_AT["gate_row1"])
            ada = 10
            steps = len(FGROUPS) * NT
            for s in range(steps + 1):
                if s >= 1:
                    for _ in range(ADA_STEPS[s - 1]):
                        add_partitions(ada)
                        ada += 1
                g, t = s // NT, s % NT
                if s < steps:
                    width = FGROUPS[g][1]
                    slot = arrived(pe, UNIT_AT["gate", g])
                    if s:
                        pe.wait_ge(silu_ready, s)
                    product(GATE_B, u_f, t, slot, width).then_inc(gate_full, 1)
                if s >= 1:
                    pe.wait_ge(h_ready, s)
                    if s >= 2:
                        pe.wait_ge(hf_ready, s - 1)
                    nk = FGROUPS[(s - 1) // NT][1] // P
                    for j in range(nk):
                        ins = pe.transpose(TURN_B[:, j * P:(j + 1) * P], h_t[:, j * P:(j + 1) * P], ident[:])
                    ins.then_inc(hturn_full, 1)
                if s < steps:
                    slot = arrived(pe, UNIT_AT["up", g])
                    product(UP_B, u_f, t, slot, width).then_inc(up_full, 1)
                else:
                    pe.wait_ge(silu_ready, steps)
                    gate_row_product(1)
                if s >= 1:
                    g, t = (s - 1) // NT, (s - 1) % NT
                    slot = arrived(pe, UNIT_AT["down", g])
                    pe.wait_ge(hf_ready, s)
                    if s <= NT:
                        pe.wait_ge(y_read, NT)
                    for k in range(nk):
                        for half in range(2):
                            ins = pe.matmul(Y_B[2 * t + half][:], h_f[:, k, :],
                                            tall(slot)[:, k, half * W:(half + 1) * W],
                                            start=(g == 0 and k == 0),
                                            stop=(g == len(FGROUPS) - 1 and k == nk - 1))
                    ins.then_inc(down_done, 1)
            turn_x(2)

            pe.wait_ge(pair_free, PAIR_AT["rec"])

            def turn_stage(i):
                pe.wait_ge(pair_free, PAIR_AT["rec"] + i + 1)
                if i:
                    pe.wait_ge(recturn_read, i)
                src = h_t[:] if i % 2 == 0 else h_f[:].rearrange("p k s -> p (k s)")
                turn_four(TURN_B, lambda j: src[:, j * P:(j + 1) * P]).then_inc(recturn_full, 1)

            for u in range(8):
                s = arrived(pe, UNIT_AT["rec", u])
                for t in range(NT):
                    product(claim(), u_f, t, s).then_inc(pair_full, 1)
                    i = NT * u + t
                    if 1 <= i <= 4 * NT:
                        turn_stage(i - 1)
            pe.wait_ge(decs_ready, 3)
            for j in range(4):
                t, half = j // 2, j % 2
                turn_four(claim(), lambda i: buf_b[:, 4 * half + i, t * P:(t + 1) * P]).then_inc(pair_full, 1)
            pe.wait_ge(pair_free, PAIR_AT["intra"])
            pe.wait_ge(y_read, 2 * NT)
            for i in range(NH + 1):
                if i < NH:
                    h = i
                    b = claim()
                    for t in range(NT):
                        ts = slice(t * P, (t + 1) * P)
                        ins = pe.matmul(b[:, ts], buf_c[:, h, ts], big_a[:, h, ts], start=True, stop=True)
                    ins.then_inc(pair_full, 1)
                    if h:
                        pe.wait_ge(states_ready, h)
                    for j in range(3):
                        rows = slice(j % 2 * CHUNK, (j % 2 + 1) * CHUNK)
                        ins = pe.matmul(kv_products[j], ks_t[rows, j // 2, h * P:(h + 1) * P],
                                        v_t[rows, j // 2, h * P:(h + 1) * P], start=True, stop=True)
                    ins.then_inc(kv_full, 1)
                if i >= 1:
                    h = i - 1
                    pe.wait_ge(pair_free, PAIR_AT["intra"] + h + 1)
                    pe.wait_ge(states_ready, h + 1)
                    hs = slice(h % 4 * P, (h % 4 + 1) * P)
                    for t in range(NT):
                        b = Y_B[2 * t + h // 4]
                        for ch in range(2 * t, 2 * t + 2):
                            rows = slice(ch % 2 * CHUNK, (ch % 2 + 1) * CHUNK)
                            ins = pe.matmul(b[rows, hs], intra[:, h % 2, ch * CHUNK:(ch + 1) * CHUNK],
                                            v_t[:, t, h * P:(h + 1) * P], start=True, stop=(ch == 0))
                            if ch:
                                ins = pe.matmul(b[rows, hs], big_a[:, h, ch * CHUNK:(ch + 1) * CHUNK],
                                                states[:, h % 2, ch - 1, :], start=False, stop=True)
                        ins.then_inc(o_full, 1)
            for t in range(NT):
                pe.wait_ge(o_gated, t + 1)
                for half in range(2):
                    turn_four(claim(), lambda j: tok[:, t, (4 * half + j) * P:(4 * half + j + 1) * P])\
                        .then_inc(pair_full, 1)
            pe.wait_ge(pair_free, PAIR_AT["gate_row2"])
            pe.wait_ge(sq_ready, 2 * NT)
            for u in range(2):
                s = arrived(pe, UNIT_AT["rwo", u])
                for t in range(NT):
                    product(Y_B[2 * t + u], o_f, t, s).then_inc(y_full, 1)
                if u == 0:
                    gate_row_product(2)
            turn_x(3)

            pe.wait_ge(pair_free, PAIR_AT["gate_row3"])
            for t in range(NT):
                for k in range(KD):
                    ins = pe.matmul(TURN_B[:, t * NE:(t + 1) * NE], u_f[:, k, t * P:(t + 1) * P], wr[:, k, :],
                                    start=(k == 0), stop=(k == KD - 1))
            ins.then_inc(logits_full, 1)
            gate_row_product(3)
            pe.wait_ge(masks_ready, 1)
            mask = [rt[:, t, 6, :] for t in range(NT)]
            pe.matmul(SMALL_B[:, 0:NE], before[:], mask[0], start=True, stop=True)
            pe.matmul(SMALL_B[:, NE:2 * NE], before[:], mask[1], start=True, stop=False)
            pe.matmul(SMALL_B[:, NE:2 * NE], ones[:], mask[0], start=False, stop=True)
            pe.matmul(SMALL_B[:, 2 * NE:3 * NE], ones[:], mask[0], start=True, stop=False)
            pe.matmul(SMALL_B[:, 2 * NE:3 * NE], ones[:], mask[1], start=False, stop=True).then_inc(places_full, 1)

            def experts(p):
                me = moe_sems[p]

                def gather(e, half):
                    for j in range(4):
                        k = 4 * half + j
                        for t in range(NT):
                            ins = pe.matmul(SMALL_B[:, j * P:(j + 1) * P], x_t[:, t, k * P:(k + 1) * P],
                                            pick[:, bass.ds(e * SEQ + t * P, P)], start=(t == 0), stop=(t == NT - 1))
                    ins.then_inc(me["pick_full"], 1)

                def scatter(event):
                    pe.wait_ge(me["put_ready"], event + 1)
                    for n in range(4):
                        t, half = n // 2, n % 2
                        if n >= 2:
                            pe.wait_ge(me["put_added"], event * 4 + (n - 1))
                        pe.matmul(Y_B[2 + n % 2][:], put[:, t * P:(t + 1) * P], ye[:, half * W:(half + 1) * W],
                                  start=True, stop=True).then_inc(me["put_full"], 1)

                def turn_h(steps_done, g):
                    pe.wait_ge(me["h_ready"], steps_done)
                    turn_four(TURN_B, lambda j: h_t[:, j * P:(j + 1) * P]).then_inc(me["hturn_full"], 1)

                pe.wait_ge(me["picks_ready"], 1)
                for j in range(4):
                    turn_four(claim(), lambda i: put_raw[:, (4 * j + i) * P:(4 * j + i + 1) * P]).then_inc(pair_full, 1)
                gather(0, 0)
                pe.wait_ge(me["ue_ready"], 1)
                gather(0, 1)
                pe.wait_ge(pair_free, PAIR_AT["turn_put"] + 4 * (p + 1))
                with pe.Fori(0, NE // 2) as pr:
                    for r in range(2):
                        def slot_of(kind, g):
                            i = EXPERT_AT[kind, g]
                            n = MOE0 + (p * NE + r) * UNITS_PER_EXPERT + i
                            pe.wait_ge(slot_filled[n % SLOTS],
                                       pr * (32 * UNITS_PER_EXPERT // SLOTS) + 16 * (n // SLOTS + 1))
                            return n % SLOTS

                        def down(g):
                            slot = slot_of("down", g)
                            pe.wait_ge(me["hf_ready"], pr * (2 * EGROUPS) + (r * EGROUPS + g + 1))
                            if g == 0:
                                pe.wait_ge(me["ye_ready"], pr * 4 + (2 * r + 1))
                            for k in range(4):
                                for half in range(2):
                                    ins = pe.matmul(Y_B[half][:], h_f[:, k, :],
                                                    tall(slot)[:, k, half * W:(half + 1) * W],
                                                    start=(g == 0 and k == 0), stop=(g == EGROUPS - 1 and k == 3))
                            ins.then_inc(me["down_done"], 1)

                        pe.wait_ge(me["ue_ready"], pr * 4 + 2 * (r + 1))
                        for g in range(EGROUPS):
                            done = pr * (2 * EGROUPS) + (r * EGROUPS + g)
                            slot = slot_of("gate", g)
                            if g >= 1:
                                pe.wait_ge(me["silu_ready"], done)
                            product(GATE_B, ue_f[:, r], 0, slot).then_inc(me["gate_full"], 1)
                            if g >= 1:
                                turn_h(done, g - 1)
                            slot = slot_of("up", g)
                            product(UP_B, ue_f[:, r], 0, slot).then_inc(me["up_full"], 1)
                            if g >= 1:
                                down(g - 1)
                            if g in (2, 4):
                                half = g // 2 - 1
                                pe.wait_ge(me["ue_ready"], pr * 4 + (2 * r + 2 + half))
                                gather(pr * 2 + (r + 1), half)
                        turn_h(pr * (2 * EGROUPS) + (r + 1) * EGROUPS, EGROUPS - 1)
                        scatter(pr * 2 + r)
                        down(EGROUPS - 1)
                pe.wait_ge(me["ye_ready"], 2 * NE + 1)
                scatter(NE)

            experts(0)
            pe.wait_ge(flag_ready, 1)
            overflow = pe.value_load(flag[0:1, 0:1], min_val=0, max_val=1)
            with pe.If(overflow > 0):
                experts(1)

        @block.vector
        def _(dve):
            n = [0]

            def step(ins):
                n[0] += 1
                ins.then_inc(dve_step, 1)

            def settled():
                dve.wait_ge(dve_step, n[0])

            dve.wait_ge(rows_turned, 1)
            dve.wait_ge(c_ready, 1)
            step(dve.tensor_copy(lbc[:, 0:2, :].rearrange("p l k -> p (l k)"), SMALL_B[:, KD:3 * KD]))
            dve.tensor_copy(normc[:], SMALL_B[:, 3 * KD:4 * KD]).then_inc(rows_read, 1)

            def ada_unit(a):
                slot = arrived(dve, UNIT_AT["ada", a])
                if a >= 2:
                    dve.wait_ge(ada_cols_full, a - 1)
                dst = acc[:, a % 2, :]
                step(dve.tensor_scalar(dst, wide(slot)[:, 0, :], ccol[:, 0:1], None, ALU.mult))
                for k in range(1, KD):
                    settled()
                    ins = dve.scalar_tensor_tensor(out=dst, in0=wide(slot)[:, k, :], scalar=ccol[:, k:k + 1], in1=dst,
                                                   op0=ALU.mult, op1=ALU.add)
                    if k < KD - 1:
                        step(ins)
                ins.then_inc(ada_summed, 1)

            def ada_read(a):
                layer, vec, half = a // ADA_UNITS, a % ADA_UNITS // 2, a % 2
                dve.wait_ge(ada_cols_full, a + 1)
                dve.tensor_scalar(modc[:, layer, vec * KD + 4 * half:vec * KD + 4 * half + 4], SMALL_B[:, 0:4],
                                  0.0 if vec % 3 == 0 else 1.0, None, ALU.add).then_inc(ada_cols_read, 1)

            def make_diag(stage):
                layer, vec = stage // 2, 2 + 3 * (stage % 2)
                dve.wait_ge(ada_cols_read, layer * ADA_UNITS + 2 * vec + 2)
                for k in range(KD):
                    ins = dve.tensor_scalar(diags[stage][:, k * P:(k + 1) * P], ident[:],
                                            modc[:, layer, vec * KD + k:vec * KD + k + 1], None, ALU.mult)
                ins.then_inc(diag_ready, 1)

            def norm(stage):
                dve.wait_ge(pair_free, PAIR_AT[f"gate_row{stage}"] + 2)
                dve.wait_ge(ln_rows, 32 * (stage + 1))
                for t in range(NT):
                    st = stat[:, t, :]
                    if stage == 0 or stage == 2:
                        dve.wait_ge(y_full, 2 * stage + 3 + t)
                    if stage == 1:
                        dve.wait_ge(down_done, len(FGROUPS) * NT - 1 + t)
                    for half in range(2):
                        hs = slice(half * W, (half + 1) * W)
                        y = y_t[:, t, hs] if stage == 3 else Y_B[2 * t + half][:]
                        ins = dve.tensor_tensor(y_t[:, t, hs], y, gate_row[:, hs], ALU.mult)
                        if half == 0 or stage == 3:
                            step(ins)
                        else:
                            ins.then_inc(y_read, 1)
                    settled()
                    if stage < 3:
                        dve.wait_ge(y_read, NT * stage + t + 1)
                    step(dve.scalar_tensor_tensor(out=y_t[:, t, :], in0=x_t[:, t, :], scalar=ALPHA, in1=y_t[:, t, :],
                                                  op0=ALU.mult, op1=ALU.add))
                    settled()
                    for half in range(2):
                        step(dve.bn_stats(st[:, 6 * half:6 * half + 6], y_t[:, t, half * W:(half + 1) * W]))
                    settled()
                    step(dve.bn_aggr(st[:, 12:14], st[:, 0:12]))
                    settled()
                    dve.tensor_scalar(st[:, 13:14], st[:, 13:14], LN_EPS, None, ALU.add).then_inc(var_ready, 1)
                    dve.wait_ge(std_ready, NT * stage + t + 1)
                    step(dve.reciprocal(st[:, 15:16], st[:, 14:15]))
                    settled()
                    step(dve.tensor_scalar(x_t[:, t, :], y_t[:, t, :], st[:, 12:13], st[:, 15:16],
                                           ALU.subtract, ALU.mult))
                    settled()
                    step(dve.tensor_tensor(x_t[:, t, :], x_t[:, t, :], g_row, ALU.mult))
                    settled()
                    dve.tensor_tensor(x_t[:, t, :], x_t[:, t, :], b_row, ALU.add).then_inc(x_ready, 1)

            dve.wait_ge(c_ready, 1)
            dve.wait_ge(consts_ready, 1)
            ada_unit(0)
            for a in range(1, 5):
                ada_unit(a)
                ada_read(a - 1)

            dve.wait_ge(smalls_loaded, 16 * 6)
            step(dve.tensor_copy(pos_f[:], pos_i[:]))
            settled()
            for t in range(NT):
                step(dve.tensor_scalar(ang[:, 0, t, :], invf[:], pos_f[:, t:t + 1], None, ALU.mult))
            settled()
            step(dve.tensor_scalar(ang[:, 2], ang[:, 0], 1.0 / TWO_PI, None, ALU.mult))
            step(dve.tensor_scalar(ang[:, 3], ang[:, 0], 1.0 / TWO_PI, 0.25, ALU.mult, ALU.add))
            settled()
            step(dve.tensor_scalar(ang[:, 2:4], ang[:, 2:4], ROUND, None, ALU.add))
            settled()
            step(dve.tensor_scalar(ang[:, 2:4], ang[:, 2:4], ROUND, None, ALU.subtract))
            settled()
            step(dve.tensor_copy(ang[:, 1], ang[:, 0]))
            settled()
            for part in (PI_1, PI_2, PI_3):
                step(dve.scalar_tensor_tensor(out=ang[:, 0:2].rearrange("p a t j -> p (a t j)"),
                                              in0=ang[:, 2:4].rearrange("p a t j -> p (a t j)"), scalar=-part,
                                              in1=ang[:, 0:2].rearrange("p a t j -> p (a t j)"),
                                              op0=ALU.mult, op1=ALU.add))
                settled()
            step(dve.tensor_scalar(ang[:, 1], ang[:, 1], float(np.pi / 2), None, ALU.add))
            settled()
            dve.tensor_scalar(ang[:, 2:4], ang[:, 0:2], PI_F, -PI_F, ALU.min, ALU.max).then_inc(angles_ready, 1)
            l0, l1, m, e0, e1, total, inv, both = (lbc[:, i, :] for i in range(8))
            step(dve.tensor_tensor(m, l0, l1, ALU.max))
            settled()
            step(dve.tensor_tensor(l0, l0, m, ALU.subtract))
            dve.tensor_tensor(l1, l1, m, ALU.subtract).then_inc(lb_logits_ready, 1)
            ada_unit(5)
            ada_read(4)
            dve.wait_ge(lb_exp_ready, 1)
            step(dve.tensor_tensor(total, e0, e1, ALU.add))
            settled()
            step(dve.reciprocal(inv, total))
            settled()
            step(dve.tensor_tensor(e0, e0, inv, ALU.mult))
            step(dve.tensor_tensor(e1, e1, inv, ALU.mult))
            settled()
            step(dve.tensor_tensor(both, e0, e1, ALU.add))
            settled()
            lb, one_less = l0, l1
            step(dve.tensor_tensor(lb, both, e0, ALU.subtract))
            settled()
            step(dve.tensor_scalar(one_less, lb, -1.0, 1.0, ALU.mult, ALU.add))
            ada_unit(6)
            ada_read(5)

            dve.wait_ge(sincos_ready, 1)
            dve.wait_ge(pair_free, PAIR_AT["qk"] + 8)
            for t in range(NT):
                heads = tok[:, t, 0:2 * D].rearrange("p (h d) -> p h d", d=HD)
                t1, t2 = heads[:, :, 0:HALF], heads[:, :, HALF:ROPE]
                sin = ang[:, 2, t, :].unsqueeze(1).to_broadcast([P, 2 * NH, HALF])
                cos = ang[:, 3, t, :].unsqueeze(1).to_broadcast([P, 2 * NH, HALF])
                tmp = [flat_d[:, (4 * t + i) * 256:(4 * t + i + 1) * 256].rearrange("p (h j) -> p h j", j=HALF)
                       for i in range(4)]
                for i, (a, b) in enumerate(((t1, cos), (t2, sin), (t2, cos), (t1, sin))):
                    step(dve.tensor_tensor(tmp[i], a, b, ALU.mult))
                settled()
                step(dve.tensor_tensor(t1, tmp[0], tmp[1], ALU.subtract))
                dve.tensor_tensor(t2, tmp[2], tmp[3], ALU.add).then_inc(rotated, 1)
            ada_read(6)
            for a in (7, 8, 9):
                ada_unit(a)
                ada_read(a)
            make_diag(0)

            for i in range(NH + 1):
                if i < NH:
                    r = i % 2
                    dve.wait_ge(pair_full, PAIR_AT["scores"] + i + 1)
                    b = PAIR[(PAIR_AT["scores"] + i) % 2]
                    for col in (0, 2 * P):
                        step(dve.copy_predicated(b[:, col:col + P], future[:], neg[:, 0:1].to_broadcast([P, P])))
                    settled()
                    step(dve.tensor_reduce(sm[:, r, 0:1], b[:, 0:P], AX.X, ALU.max))
                    step(dve.tensor_reduce(sm[:, r, 1:2], b[:, P:3 * P], AX.X, ALU.max))
                    settled()
                    dve.tensor_scalar(sm[:, r, 2:4], sm[:, r, 0:2], -SCALE, None, ALU.mult).then_inc(row_max_ready, 1)
                if i >= 1:
                    h, r = i - 1, (i - 1) % 2
                    dve.wait_ge(pair_free, PAIR_AT["scores"] + h + 1)
                    step(dve.reciprocal(sm[:, r, 6:8], sm[:, r, 4:6]))
                    settled()
                    step(dve.tensor_scalar(probs[:, r, 0:P], probs[:, r, 0:P], sm[:, r, 6:7], None, ALU.mult))
                    dve.tensor_scalar(probs[:, r, P:3 * P], probs[:, r, P:3 * P], sm[:, r, 7:8], None, ALU.mult)\
                       .then_inc(probs_ready, 1)
            norm(0)

            ada = 10
            for s in range(len(FGROUPS) * NT):
                width = FGROUPS[s // NT][1]
                dve.wait_ge(silu_ready, s + 1)
                dve.wait_ge(up_full, s + 1)
                dve.tensor_tensor(h_t[:, 0:width], h_t[:, 0:width], UP_B[:, 0:width], ALU.mult).then_inc(h_ready, 1)
                for _ in range(ADA_STEPS[s]):
                    if ada > 10:
                        ada_read(ada - 1)
                    ada_unit(ada)
                    ada += 1
                if s == 2:
                    make_diag(1)
            ada_read(ada - 1)
            norm(1)

            for i in range(4 * NT):
                u, t = i // NT, i % NT
                dve.wait_ge(recturn_full, i + 1)
                dst = (big_a if u < 2 else buf_b)[:, u % 2 * 4:u % 2 * 4 + 4, t * P:(t + 1) * P]
                dve.tensor_copy(dst, TURN_B[:].rearrange("p (k s) -> p k s", k=4)).then_inc(recturn_read, 1)
            dve.wait_ge(recturn_read, 4 * NT)
            for k in range(KD):
                step(dve.tensor_scalar(buf_c[:, k, :], buf_b[:, k, :], one_less[:, k:k + 1], lb[:, k:k + 1],
                                       ALU.mult, ALU.add))
            settled()
            dve.tensor_scalar(buf_b[:], buf_c[:], -1.0, 1.0, ALU.mult, ALU.add).then_inc(fgate_ready, 1)
            dve.wait_ge(logf_ready, 1)
            for h in range(NH):
                step(dve.tensor_tensor_scan(buf_d[:, h, :], carry[:], buf_c[:, h, :], 0.0, ALU.mult, ALU.add))
            settled()
            dve.tensor_copy(last[:, 0], buf_d[:].rearrange("p h (j c) -> p h j c", c=CHUNK)[:, :, :, CHUNK - 1])\
               .then_inc(gcum_ready, 1)
            dve.wait_ge(expg_ready, 2)
            dve.tensor_tensor(big_a[:], big_a[:], buf_c[:], ALU.mult).then_inc(expg_used, 1)
            dve.wait_ge(expng_ready, 1)
            dve.tensor_tensor(buf_c[:], buf_b[:], buf_c[:], ALU.mult).then_inc(decs_ready, 1)
            dve.wait_ge(expst_ready, 3 * NH)
            dve.wait_ge(decs_ready, 1)
            dve.tensor_tensor(buf_b[:, :, 0:3 * CHUNK], buf_b[:, :, 0:3 * CHUNK], buf_d[:, :, 0:3 * CHUNK], ALU.mult)\
               .then_inc(decs_ready, 1)
            dve.wait_ge(decs_ready, 2)
            dve.memset(intra, 0.0).then_inc(decs_ready, 1)
            dve.wait_ge(decs_ready, 3)
            for h in range(NH):
                r = h % 2
                if h >= 2:
                    dve.wait_ge(o_full, NT * (h - 1))
                dve.wait_ge(pair_full, PAIR_AT["intra"] + h + 1)
                dve.copy_predicated(intra[:, r, :], keep[:].rearrange("p t c -> p (t c)"),
                                    PAIR[(PAIR_AT["intra"] + h) % 2][:, 0:SEQ]).then_inc(pair_free, 1)
                dve.wait_ge(kv_full, h + 1)
                step(dve.tensor_copy(states[:, r, 0, :], kv_products[0]))
                for j in (1, 2):
                    settled()
                    ins = dve.scalar_tensor_tensor(out=states[:, r, j, :], in0=states[:, r, j - 1, :],
                                                   scalar=last[:, 1, h, j:j + 1], in1=kv_products[j],
                                                   op0=ALU.mult, op1=ALU.add)
                    if j == 1:
                        step(ins)
                ins.then_inc(states_ready, 1)
            dve.wait_ge(o_ready, 2 * NT)
            for t in range(NT):
                dve.wait_ge(sq_ready, 2 * (t + 1))
                step(dve.tensor_reduce(rms[:, t, 0, :], tok[:, t, D:2 * D].rearrange("p (h d) -> p h d", d=HD),
                                       AX.X, ALU.add))
                settled()
                dve.tensor_scalar(rms[:, t, 0, :], rms[:, t, 0, :], 1.0 / HD, RMS_EPS, ALU.mult, ALU.add)\
                   .then_inc(msq_ready, 1)
            for t in range(NT):
                dve.wait_ge(rms_ready, t + 1)
                step(dve.reciprocal(rms[:, t, 0, :], rms[:, t, 1, :]))
                settled()
                heads = tok[:, t, 0:D].rearrange("p (h d) -> p h d", d=HD)
                step(dve.tensor_tensor(heads, heads, rms[:, t, 0, :].unsqueeze(2).to_broadcast([P, NH, HD]), ALU.mult))
                settled()
                dve.tensor_tensor(tok[:, t, 0:D], tok[:, t, 0:D], y_t[:, t, :], ALU.mult).then_inc(o_gated, 1)
            dve.wait_ge(o_gated, NT)
            make_diag(2)
            norm(2)

            dve.wait_ge(logits_full, 1)
            make_diag(3)
            step(dve.tensor_copy(rt[:, :, 0, :], TURN_B[:, 0:NT * NE].rearrange("p (t e) -> p t e", t=NT)))
            settled()
            for t in range(NT):
                logit, top, idx, first, second, w, mask, comb = (rt[:, t, i, :] for i in range(8))
                step(dve.max(top, logit))
                settled()
                step(dve.max_index(ridx[:, t, :], top, logit))
                dve.tensor_tensor(w[:, 0:1], top[:, 1:2], top[:, 0:1], ALU.subtract).then_inc(gap_ready, 1)
                settled()
                step(dve.tensor_copy(idx[:, 0:2], ridx[:, t, 0:2]))
                settled()
                step(dve.tensor_scalar(first, iota[:, 0:NE], idx[:, 0:1], None, ALU.is_equal))
                step(dve.tensor_scalar(second, iota[:, 0:NE], idx[:, 1:2], None, ALU.is_equal))
                dve.wait_ge(gap_exp, t + 1)
                step(dve.tensor_scalar(w[:, 3:4], w[:, 2:3], 1.0, None, ALU.add))
                settled()
                step(dve.reciprocal(w[:, 4:5], w[:, 3:4]))
                settled()
                step(dve.tensor_tensor(w[:, 5:6], w[:, 2:3], w[:, 4:5], ALU.mult))
                step(dve.tensor_scalar(comb, first, w[:, 4:5], None, ALU.mult))
                settled()
                step(dve.scalar_tensor_tensor(out=comb, in0=second, scalar=w[:, 5:6], in1=comb,
                                              op0=ALU.mult, op1=ALU.add))
                ins = dve.tensor_tensor(mask, first, second, ALU.add)
                if t < NT - 1:
                    step(ins)
            ins.then_inc(masks_ready, 1)
            settled()
            dve.wait_ge(places_full, 1)
            step(dve.tensor_copy(rt[:, :, 0, :], SMALL_B[:, 0:NT * NE].rearrange("p (t e) -> p t e", t=NT)))
            step(dve.tensor_reduce(over[:, 0:1], SMALL_B[:, NT * NE:(NT + 1) * NE], AX.X, ALU.max))
            settled()
            dve.tensor_scalar(flag[:], over[:, 0:1], float(CAP), None, ALU.is_gt).then_inc(flag_ready, 1)
            step(dve.memset(y_t[:], 0.0))
            step(dve.memset(pick[:, NE * SEQ:(NE + 1) * SEQ], 0.0))
            step(dve.memset(put_all[:, 0:SEQ], 0.0))
            step(dve.memset(ye, 0.0))
            settled()

            def experts(p):
                me = moe_sems[p]
                for e in range(NE):
                    for t in range(NT):
                        cols = slice(e * SEQ + t * P, e * SEQ + (t + 1) * P)
                        slots = iota[:, p * CAP:(p + 1) * CAP]
                        dve.tensor_scalar(pick[:, cols], slots, rt[:, t, 0, e:e + 1], rt[:, t, 6, e:e + 1],
                                          ALU.is_equal, ALU.mult)
                        ins = dve.tensor_scalar(put_raw[:, cols], slots, rt[:, t, 0, e:e + 1], rt[:, t, 7, e:e + 1],
                                                ALU.is_equal, ALU.mult)
                ins.then_inc(me["picks_ready"], 1)

                def next_put(event):
                    dve.tensor_copy(put, put_all[:, bass.ds(event * SEQ, SEQ)]).then_inc(me["put_ready"], 1)

                def add_outputs(event):
                    for i in range(4):
                        t, half = i // 2, i % 2
                        dve.wait_ge(me["put_full"], event * 4 + (i + 1))
                        dst = y_t[:, t, half * W:(half + 1) * W]
                        dve.tensor_tensor(dst, dst, Y_B[2 + i % 2][:], ALU.add).then_inc(me["put_added"], 1)
                    dve.wait_ge(me["put_added"], event * 4 + 4)

                dve.wait_ge(pair_free, PAIR_AT["turn_put"] + 4 * (p + 1))
                with dve.Fori(0, NE // 2) as pr:
                    for r in range(2):
                        for g in range(EGROUPS):
                            done = pr * (2 * EGROUPS) + (r * EGROUPS + g)
                            dve.wait_ge(me["silu_ready"], done + 1)
                            dve.wait_ge(me["up_full"], done + 1)
                            dve.tensor_tensor(h_t[:], h_t[:], UP_B[:], ALU.mult).then_inc(me["h_ready"], 1)
                            if g == 3:
                                next_put(pr * 2 + r)
                        add_outputs(pr * 2 + r)
                next_put(NE)
                add_outputs(NE)

            experts(0)
            overflow = dve.value_load(flag[0:1, 0:1], min_val=0, max_val=1)
            with dve.If(overflow > 0):
                experts(1)
            norm(3)


_INS = ["x", "c", "positions", "ada_w", "ada_b", "ln_g", "ln_b", "attn_w_in", "attn_w_out", "rec_w_in",
        "rec_lb_logits", "rec_norm_w", "rec_w_out", "ffn_w_gate", "ffn_w_up", "ffn_w_down", "router_w",
        "moe_w_gate", "moe_w_up", "moe_w_down"]


def kernel(**inputs):
    import concourse.bacc as bacc
    from concourse.bass_utils import run_bass_kernel_spmd

    nc = bacc.Bacc("TRN2", target_bir_lowering=False, num_devices=1)
    arrays, args = {}, []
    for name in _INS:
        a = np.ascontiguousarray(inputs[name])
        arrays[f"in_{name}"] = a
        args.append(nc.dram_tensor(f"in_{name}", a.shape, mybir.dt.from_np(a.dtype), kind="ExternalInput").ap())
    out = nc.dram_tensor("out", (1, SEQ, D), F32, kind="ExternalOutput").ap()
    trunk_kernel(nc, *args, out)
    r = run_bass_kernel_spmd(nc, [arrays], core_ids=[0])
    return r.results[0]["out"]
```

```python
from contextlib import ExitStack

import numpy as np
import concourse.bass as bass
from concourse import mybir

ALU = mybir.AluOpType
ACT = mybir.ActivationFunctionType
AX = mybir.AxisListType
F32 = mybir.dt.float32
F32R = mybir.dt.float32r
I32 = mybir.dt.int32
U32 = mybir.dt.uint32
U8 = mybir.dt.uint8
BF16 = mybir.dt.bfloat16

P = 128
D = 1024
SEQ = 256
NT = SEQ // P
KD = D // P
W = 512
NH = 8
HD = 128
ROPE = HD // 4
HALF = ROPE // 2
ROPE_THETA = 500000.0
CHUNK = 64
D_FF = 2816
NE = 8
D_FFE = 3584
DEPTH = 2
ALPHA = (2.0 * DEPTH) ** 0.25
LN_EPS = 1e-5
RMS_EPS = 1e-6
CAP = 128
SLOTS = 6
SPLITS = 4
PART = 2048
SCALE = HD ** -0.5
MASKED = -3.0e38

FGROUPS = [(g * W, min(W, D_FF - g * W)) for g in range(-(-D_FF // W))]
EGROUPS = D_FFE // W
ADA_UNITS = 6 * D // W
PARTS_PER_EXPERT = 6 * EGROUPS
PARTS_PER_PAIR = 2 * PARTS_PER_EXPERT
ADA_IN_REC = 10 + 2 * len(FGROUPS)
assert ADA_IN_REC + 2 == DEPTH * ADA_UNITS

TWO_PI = 2.0 * np.pi
PI_1 = 6.28125
PI_2 = float(np.float32(np.round((TWO_PI - PI_1) * 2.0 ** 20) / 2.0 ** 20))
PI_3 = float(np.float32(TWO_PI - PI_1 - PI_2))
ROUND = 1.5 * 2.0 ** 23
PI_F = float(np.float32(3.1415925))


def plan_stream():
    s = [("ada", j) for j in range(4)]
    s += [("qkv", 0), ("qkv", 1), ("ada", 4), ("qkv", 2), ("ada", 5), ("qkv", 3), ("ada", 6),
          ("qkv", 4), ("ada", 7), ("qkv", 5), ("ada", 8), ("ada", 9), ("wo", 0), ("wo", 1)]
    for g in range(len(FGROUPS)):
        s += [("gate", g), ("ada", 10 + 2 * g), ("up", g), ("ada", 11 + 2 * g), ("down", g)]
    s += [("rec", 0), ("ada", ADA_IN_REC), ("rec", 1), ("ada", ADA_IN_REC + 1)] + [("rec", n) for n in range(2, 8)]
    return s + [("rwo", 0), ("rwo", 1)]


def parts_of(unit):
    return 1 if unit == ("down", len(FGROUPS) - 1) else 2


RAW = [(u, h) for u in plan_stream() for h in range(parts_of(u))]
RAW_AT = {r: i for i, r in enumerate(RAW)}
SPLIT = [r for r in RAW if r[0][0] != "ada"]
SPLIT_AT = {r: i for i, r in enumerate(SPLIT)}
RAW0, SPLIT0 = len(RAW), len(SPLIT)
FIRSTS = [sum(1 for u, h in SPLIT[:i + 1] if h == 0 and parts_of(u) == 2) for i in range(SPLIT0)]
FIRSTS0 = FIRSTS[-1]
assert PARTS_PER_EXPERT % SLOTS == 0 and PARTS_PER_PAIR % SPLITS == 0


def expert_units():
    s = [("gate", 0), ("up", 0)]
    for g in range(1, EGROUPS):
        s += [("gate", g), ("up", g), ("down", g - 1)]
    return s + [("down", EGROUPS - 1)]


EXPERT_UNITS = expert_units()
EXPERT_END = {u: 2 * i + 1 for i, u in enumerate(EXPERT_UNITS)}


def trunk_kernel(nc, x, c, positions, ada_w, ada_b, ln_g, ln_b, attn_w_in, attn_w_out, rec_w_in,
                 rec_lb_logits, rec_norm_w, rec_w_out, ffn_w_gate, ffn_w_up, ffn_w_down, router_w,
                 moe_w_gate, moe_w_up, moe_w_down, out):
    with ExitStack() as ctx:
        def sb(name, shape, dt=F32):
            return ctx.enter_context(nc.sbuf_tensor(name, shape, dt))

        def sem(name):
            return ctx.enter_context(nc.semaphore(name))

        raw = sb("raw", [P, SLOTS, PART])
        w_hi = sb("w_hi", [P, SPLITS, PART], F32R)
        w_lo = sb("w_lo", [P, SPLITS, PART], F32R)
        l_hi = sb("l_hi", [P, KD, SEQ], F32R)
        l_lo = sb("l_lo", [P, KD, SEQ], F32R)
        hf_hi = sb("hf_hi", [P, 4, P], F32R)
        hf_lo = sb("hf_lo", [P, 4, P], F32R)
        big_a = sb("big_a", [P, KD, SEQ])
        arena = sb("arena", [P, 3, KD * SEQ])
        tok = sb("tok", [P, NT, 3 * D])
        x_t = sb("x_t", [P, NT, D])
        y_t = sb("y_t", [P, NT, D])
        ident = sb("ident", [P, P])
        ones = sb("ones", [P, P])
        before = sb("before", [P, P])
        future = sb("future", [P, P], U8)
        keep = sb("keep", [P, NT, P], U8)
        neg = sb("neg", [P, 1])
        carry = sb("carry", [P, SEQ], BF16)
        iota = carry
        bias_c = sb("bias_c", [P, 4, DEPTH * ADA_UNITS])
        ccol = sb("ccol", [P, KD])
        modc = sb("modc", [P, DEPTH, 6 * KD])
        pos_i = sb("pos_i", [P, NT], I32)
        pos_f = sb("pos_f", [P, NT])
        lbc = sb("lbc", [P, 8, KD])
        normc = sb("normc", [P, KD])
        stat = sb("stat", [P, NT, 16])
        rms = sb("rms", [P, NT, 2, NH])
        sm = rms[:, :, 0, :]
        last = lbc[:, :, :].rearrange("p (a b) k -> p a (b k)", a=2).rearrange("p a (h j) -> p a h j", j=4)
        ridx = sb("ridx", [P, NT, 8], U32)
        over, flag = pos_f, pos_i[:, 0:1]
        h_t = tok[:, 1, D:2 * D].rearrange("p (b n) -> p b n", b=2)
        c_rows = tok[0:KD, 0, 0:P]
        lb_rows = tok[0:DEPTH * KD, 0, P:2 * P]
        nw_rows = tok[0:KD, 0, 2 * P:3 * P]
        ab_rows = tok[0:DEPTH * ADA_UNITS, 1, 0:W]
        keep_raw = tok[:, 1, D:D + NT * P].rearrange("p (t c) -> p t c", t=NT)

        bank = [ctx.enter_context(nc.psum_tensor(f"bank{i}", [P, W], F32)) for i in range(8)]
        PAIR = bank[0:2]
        GATE_B, UP_B, TURN_B, SMALL_B = bank[0:4]
        Y_B = bank[4:8]

        buf_b, buf_c, buf_d = (arena[:, i, :].rearrange("p (k s) -> p k s", k=KD) for i in range(3))
        q_f, k_f = big_a, buf_b
        flat_d = arena[:, 2, :]
        probs = flat_d[:, 0:768].rearrange("p (b n) -> p b n", b=2)
        probs_f = flat_d[:, 768:1536].rearrange("p (b n) -> p b n", b=2)
        ang = flat_d[:, 1536:1536 + 4 * NT * HALF].rearrange("p (a t j) -> p a t j", a=4, t=NT)
        invf = flat_d[:, 1536 + 4 * NT * HALF:1536 + (4 * NT + 1) * HALF]
        v_t = tok[:, :, 2 * D:3 * D]
        gate_row = tok[:, 0, D:2 * D]
        g_row = tok[:, 0, 0:D]
        b_row = tok[:, 1, 0:D]
        flat_all = arena[:, :, :].rearrange("p a n -> p (a n)")
        pick = flat_all[:, 0:(NE + 1) * SEQ]
        put_all = flat_all[:, (NE + 1) * SEQ:(2 * NE + 2) * SEQ]
        ye = flat_all[:, (2 * NE + 2) * SEQ:(2 * NE + 2) * SEQ + D]
        put = flat_all[:, (2 * NE + 2) * SEQ + D:(2 * NE + 3) * SEQ + D]
        free = (2 * NE + 3) * SEQ + D
        rt = flat_all[:, free:free + NT * 8 * NE].rearrange("p (t i e) -> p t i e", t=NT, i=8)
        wr = flat_all[:, free + NT * 8 * NE:free + NT * 8 * NE + D * NE // P].rearrange("p (k e) -> p k e", e=NE)
        put_raw = tok[:, :, 2 * D:3 * D].rearrange("p a (e s) -> p a e s", e=NE // 2)
        ks_t = tok[:, :, D:2 * D]
        intra = flat_d[:, 0:2 * SEQ].rearrange("p (b s) -> p b s", b=2)
        states = flat_d[:, 2 * SEQ:2 * SEQ + 6 * HD].rearrange("p (b j n) -> p b j n", b=2, j=3)
        y_flat = y_t[:, :, :].rearrange("p t d -> p (t d)")
        acc = y_flat[:, 0:D].rearrange("p (b n) -> p b n", b=2)
        diags = [y_flat[:, D:2 * D], flat_d[:, 0:D], y_flat[:, 0:D], v_t[:, 0, :]]
        stage_rows = [tok[:, 1, i * W:(i + 1) * W] for i in range(2)]
        kv_products = [TURN_B[:, 0:P], SMALL_B[:, 0:P], TURN_B[:, P:2 * P]]
        temp_flat = big_a[:, :, :].rearrange("p k s -> p (k s)")
        ue_hi, ue_lo = (l[:, :, :].rearrange("p k s -> p (k s)").rearrange("p (b k s) -> p b k s", b=2, k=KD)
                        for l in (l_hi, l_lo))

        raw_filled = [sem(f"raw_filled{i}") for i in range(SLOTS)]
        hi_ready = sem("hi_ready")
        raw_used = sem("raw_used")
        firsts_used = sem("firsts_used")
        l_hi_ready = sem("l_hi_ready")
        l_lo_ready = sem("l_lo_ready")
        head_hi = sem("head_hi")
        hf_hi_ready = sem("hf_hi_ready")
        x_loaded = sem("x_loaded")
        smalls_loaded = sem("smalls_loaded")
        pos_loaded = sem("pos_loaded")
        wr_loaded = sem("wr_loaded")
        consts_ready = sem("consts_ready")
        iota_ready = sem("iota_ready")
        pool_step = sem("pool_step")
        dve_step = sem("dve_step")
        rows_turned = sem("rows_turned")
        c_ready = sem("c_ready")
        lb_logits_ready = sem("lb_logits_ready")
        lb_exp_ready = sem("lb_exp_ready")
        angles_ready = sem("angles_ready")
        sincos_ready = sem("sincos_ready")
        ada_cols_full = sem("ada_cols_full")
        ada_cols_read = sem("ada_cols_read")
        pair_full = sem("pair_full")
        pair_free = sem("pair_free")
        rotated = sem("rotated")
        row_max_ready = sem("row_max_ready")
        probs_ready = sem("probs_ready")
        turn_full = sem("turn_full")
        turn_free = sem("turn_free")
        head_full = sem("head_full")
        head_free = sem("head_free")
        y_full = sem("y_full")
        y_read = sem("y_read")
        diag_ready = sem("diag_ready")
        var_ready = sem("var_ready")
        std_ready = sem("std_ready")
        x_ready = sem("x_ready")
        ln_rows = sem("ln_rows")
        gate_full = sem("gate_full")
        silu_ready = sem("silu_ready")
        up_full = sem("up_full")
        h_ready = sem("h_ready")
        hturn_full = sem("hturn_full")
        hf_ready = sem("hf_ready")
        recturn_full = sem("recturn_full")
        recturn_read = sem("recturn_read")
        rows_read = sem("rows_read")
        down_done = sem("down_done")
        fgate_ready = sem("fgate_ready")
        logf_ready = sem("logf_ready")
        gcum_ready = sem("gcum_ready")
        expg_ready = sem("expg_ready")
        expg_used = sem("expg_used")
        expng_ready = sem("expng_ready")
        expst_ready = sem("expst_ready")
        decs_ready = sem("decs_ready")
        kv_full = sem("kv_full")
        states_ready = sem("states_ready")
        o_full = sem("o_full")
        o_ready = sem("o_ready")
        sq_ready = sem("sq_ready")
        msq_ready = sem("msq_ready")
        rms_ready = sem("rms_ready")
        o_gated = sem("o_gated")
        logits_full = sem("logits_full")
        gap_ready = sem("gap_ready")
        gap_exp = sem("gap_exp")
        masks_ready = sem("masks_ready")
        zeros_ready = sem("zeros_ready")
        places_full = sem("places_full")
        flag_ready = sem("flag_ready")
        out_stored = sem("out_stored")
        moe_sems = [{k: sem(f"{k}_{p}") for k in (
            "picks_ready", "pick_full", "ue_ready", "ue_hi_ready", "ue_split", "gate_full", "silu_ready", "up_full", "h_ready",
            "hturn_full", "hf_hi_ready", "hf_ready", "down_done", "ye_ready", "put_ready", "put_full", "put_added")} for p in range(2)]

        def raw_source(unit, h, e=None):
            kind, a = unit
            if e is not None:
                if kind == "down":
                    w = moe_w_down[0].rearrange("e (k p) n -> p e k n", p=P)
                    src = w[:, bass.ds(e, 1), 4 * a + 2 * h:4 * a + 2 * h + 2, :]
                else:
                    w = (moe_w_gate if kind == "gate" else moe_w_up)[0].rearrange("e (k p) n -> p e k n", p=P)
                    src = w[:, bass.ds(e, 1), 4 * h:4 * h + 4, a * W:(a + 1) * W]
                return src.rearrange("p e k n -> p (e k) n"), PART
            if kind == "down":
                lo = FGROUPS[a][0] + 2 * h * P
                return ffn_w_down[0, lo:lo + 2 * P, :].rearrange("(k p) n -> p k n", p=P), PART
            if kind in ("gate", "up"):
                lo, n = FGROUPS[a]
                w = (ffn_w_gate if kind == "gate" else ffn_w_up)[0]
            elif kind == "ada":
                lo, n, w = a % ADA_UNITS * W, W, ada_w[a // ADA_UNITS]
            else:
                w = {"qkv": attn_w_in, "wo": attn_w_out, "rec": rec_w_in, "rwo": rec_w_out}[kind][0]
                lo, n = a * W, W
            return columns(w, lo, n)[:, 4 * h:4 * h + 4, :], 4 * n

        def columns(w, lo, n):
            return w.rearrange("(k p) n -> p k n", p=P)[:, :, lo:lo + n]

        block = ctx.enter_context(nc.Block())

        PAIR_AT, n = {}, 0
        for stage, count in (("mod0", 4), ("qk", 8), ("v0", 2), ("turn_q", 4), ("v1", 2), ("turn_k", 4),
                             ("gate_row0", 2), ("scores", NH), ("mod1", 4), ("gate_row1", 2), ("mod2", 4),
                             ("rec", 16), ("turn_ks", 4), ("intra", NH), ("turn_o", 4), ("gate_row2", 2),
                             ("mod3", 4), ("gate_row3", 2), ("turn_put", 4), ("turn_put2", 4), ("end", 0)):
            PAIR_AT[stage], n = n, n + count

        def pair_bank(n):
            if n - 2 in (PAIR_AT["mod1"], PAIR_AT["mod2"]):
                return TURN_B
            if n - 3 in (PAIR_AT["mod1"], PAIR_AT["mod2"]):
                return SMALL_B
            return PAIR[n % 2]

        def pair_claim(pe, n):
            if n >= 2:
                pe.wait_ge(pair_free, n - 1)
            return pair_bank(n)

        def used(m):
            (kind, a), h = SPLIT[m]
            if h == 0 and parts_of((kind, a)) == 2:
                return firsts_used, FIRSTS[m]
            if kind == "qkv":
                first = {4: PAIR_AT["v0"], 5: PAIR_AT["v1"]}.get(a, PAIR_AT["qk"] + NT * a)
                return pair_full, first + NT
            if kind == "rec":
                return pair_full, PAIR_AT["rec"] + NT * (a + 1)
            if kind in ("wo", "rwo"):
                return y_full, (4 if kind == "rwo" else 0) + NT * (a + 1)
            return {"gate": gate_full, "up": up_full, "down": down_done}[kind], NT * (a + 1)

        EXPERT_DONE = {"gate": "gate_full", "up": "up_full", "down": "down_done"}

        def expert_used(p, pr, i):
            r, j = divmod(i, PARTS_PER_EXPERT)
            (kind, g), h = EXPERT_UNITS[j // 2], j % 2
            if h == 0:
                return firsts_used, pr * PARTS_PER_EXPERT + (
                    FIRSTS0 + p * NE * PARTS_PER_EXPERT // 2 + i // 2 + 1)
            return moe_sems[p][EXPERT_DONE[kind]], pr * (2 * EGROUPS) + (r * EGROUPS + g + 1)

        def raw_index(p, i):
            return RAW0 + p * NE * PARTS_PER_EXPERT + i

        def split_index(p, i):
            return SPLIT0 + p * NE * PARTS_PER_EXPERT + i

        class Splits:

            def __init__(self, before_experts, expert_part):
                self.next, self.before_experts, self.expert_part = 0, before_experts, expert_part

            def ahead(self, unit, more=3):
                last_part = SPLIT_AT[unit, parts_of(unit) - 1] + more
                while self.next <= last_part:
                    if self.next < SPLIT0:
                        self.before_experts(self.next)
                    else:
                        self.expert_part(0, 0, self.next - SPLIT0)
                    self.next += 1

            def start_pass(self, p):
                first = self.next - SPLIT0 if p == 0 else 0
                for i in range(first, SPLITS):
                    self.expert_part(p, 0, i)

            def start_pair(self, p, pr, final):
                self.p, self.pr, self.final, self.i = p, pr, final, SPLITS

            def ahead_in_pair(self, r, unit, more=3):
                stop = r * PARTS_PER_EXPERT + EXPERT_END[unit] + more
                if self.final:
                    stop = min(stop, PARTS_PER_PAIR - 1)
                while self.i <= stop:
                    self.expert_part(self.p, self.pr, self.i)
                    self.i += 1

        @block.sync
        def _(sp):
            sp.dma_start(c_rows, c.rearrange("b (k p) -> (b k) p", p=P)).then_inc(smalls_loaded, 16)
            sp.dma_start(lb_rows, rec_lb_logits.rearrange("l (k p) -> (l k) p", p=P)).then_inc(smalls_loaded, 16)
            sp.dma_start(nw_rows, rec_norm_w.rearrange("l (k p) -> (l k) p", p=P)).then_inc(smalls_loaded, 16)
            sp.dma_start(ab_rows, ada_b.rearrange("l (j w) -> (l j) w", w=W)).then_inc(smalls_loaded, 16)
            for i, (unit, h) in enumerate(RAW):
                if i >= SLOTS:
                    sp.wait_ge(raw_used, i - SLOTS + 1)
                src, n = raw_source(unit, h)
                dst = raw[:, i % SLOTS, 0:n].rearrange("p (k n) -> p k n", k=src.shape[1])
                sp.dma_start(dst, src).then_inc(raw_filled[i % SLOTS], 16)
                if i == 1:
                    sp.dma_start(x_t[:], x[0].rearrange("(t p) d -> p t d", p=P)).then_inc(x_loaded, 16)

            def expert_weights(p):
                with sp.Fori(0, NE) as e:
                    for j in range(PARTS_PER_EXPERT):
                        i = raw_index(p, j)
                        sp.wait_ge(raw_used, e * PARTS_PER_EXPERT + (i - SLOTS + 1))
                        src, n = raw_source(EXPERT_UNITS[j // 2], j % 2, e)
                        dst = raw[:, i % SLOTS, 0:n].rearrange("p (k n) -> p k n", k=src.shape[1])
                        sp.dma_start(dst, src).then_inc(raw_filled[i % SLOTS], 16)

            expert_weights(0)
            sp.wait_ge(flag_ready, 1)
            overflow = sp.value_load(flag[0:1, 0:1], min_val=0, max_val=1)
            with sp.If(overflow > 0):
                expert_weights(1)

        @block.gpsimd
        def _(pool):
            n = [0]

            def step(ins):
                n[0] += 1
                ins.then_inc(pool_step, 1)

            def settled():
                pool.wait_ge(pool_step, n[0])

            step(pool.memset(ident[:], 0.0))
            step(pool.memset(ones[:], 1.0))
            step(pool.memset(neg[:], MASKED))
            step(pool.memset(carry[:], 1.0))
            f = np.exp(np.float32(-np.log(ROPE_THETA)) * np.arange(HALF, dtype=np.float32) * np.float32(2.0 / ROPE))
            for j in range(HALF):
                step(pool.memset(invf[:, j:j + 1], float(np.float32(f[j]))))
            settled()
            step(pool.affine_select(out=ident[:], in_=ident[:], compare_op=ALU.not_equal, fill=1.0,
                                    base=0, pattern=[[-1, P]], channel_multiplier=1))
            step(pool.affine_select(out=before[:], in_=ones[:], compare_op=ALU.is_gt, fill=0.0,
                                    base=0, pattern=[[1, P]], channel_multiplier=-1))
            step(pool.memset(carry[:].rearrange("p (c s) -> p c s", s=CHUNK)[:, :, 0:1], 0.0))
            settled()
            step(pool.tensor_copy(future[:], before[:]))
            diag = keep_raw
            step(pool.affine_select(out=diag, in_=ones[:].unsqueeze(1).to_broadcast([P, NT, P]),
                                    compare_op=ALU.is_ge, fill=0.0,
                                    base=0, pattern=[[0, NT], [1, P]], channel_multiplier=-1))
            settled()
            for t in range(NT):
                step(pool.memset(keep_raw[0:CHUNK, t, CHUNK:P], 0.0))
            settled()
            pool.tensor_copy(keep[:], diag).then_inc(consts_ready, 1)
            pool.wait_ge(gcum_ready, 1)
            pool.iota(iota[:], pattern=[[1, 2 * CAP]], base=0, channel_multiplier=0,
                      allow_small_or_imprecise_dtypes=True).then_inc(iota_ready, 1)

        @block.scalar
        def _(act):
            pair = [0]

            def pair_take():
                act.wait_ge(pair_full, pair[0] + 1)
                pair[0] += 1
                return pair_bank(pair[0] - 1)

            def hi_part(m, raw_i, fills, buffer_free):
                act.wait_ge(raw_filled[raw_i % SLOTS], fills)
                if buffer_free:
                    act.wait_ge(*buffer_free)
                act.activation(w_hi[:, m % SPLITS, :], raw[:, raw_i % SLOTS, :], ACT.Copy).then_inc(hi_ready, 1)

            def before_experts(m):
                i = RAW_AT[SPLIT[m]]
                n = raw_source(*SPLIT[m])[1]
                act.wait_ge(raw_filled[i % SLOTS], 16 * (i // SLOTS + 1))
                if m >= SPLITS:
                    act.wait_ge(*used(m - SPLITS))
                act.activation(w_hi[:, m % SPLITS, 0:n], raw[:, i % SLOTS, 0:n], ACT.Copy).then_inc(hi_ready, 1)

            def expert_part(p, pr, i):
                n, m = raw_index(p, i), split_index(p, i)
                if i >= SPLITS:
                    free = expert_used(p, pr, i - SPLITS)
                elif p == 0:
                    free = used(m - SPLITS)
                else:
                    free = expert_used(0, NE // 2 - 1, PARTS_PER_PAIR + i - SPLITS)
                hi_part(m, n, pr * (16 * PARTS_PER_PAIR // SLOTS) + 16 * (n // SLOTS + 1), free)

            splits = Splits(before_experts, expert_part)

            with nc.allow_non_contiguous_dma(reason="256 positions, one per partition and tile"):
                act.dma_start(pos_i[:], positions.rearrange("b (t p) -> p (b t)", p=P)).then_inc(pos_loaded, 16)

            act.wait_ge(rows_turned, 1)
            act.activation(ccol[:], SMALL_B[:, 0:KD], ACT.Silu).then_inc(c_ready, 1)
            def split_left(t, half, affine, split=True):
                b = pair_take()
                for j in range(4):
                    k = 4 * half + j
                    ins = act.activation(big_a[:, k, t * P:(t + 1) * P], b[:, j * P:(j + 1) * P], **affine(k))
                ins.then_inc(pair_free, 1)
                if split:
                    act.wait_ge(pair_free, pair[0])
                    ks = slice(4 * half, 4 * half + 4)
                    act.activation(l_hi[:, ks, t * P:(t + 1) * P], big_a[:, ks, t * P:(t + 1) * P],
                                   ACT.Copy).then_inc(l_hi_ready, 1)

            def modulate(layer, vec, split=True, stage=None):
                act.wait_ge(ada_cols_read, ADA_UNITS * layer + 2 * (vec + 2))
                for t in range(NT):
                    if stage is not None:
                        deviation(stage, t)
                    for half in range(2):
                        split_left(t, half, lambda k: dict(
                            func=ACT.Identity, scale=modc[:, layer, (vec + 1) * KD + k:(vec + 1) * KD + k + 1],
                            bias=modc[:, layer, vec * KD + k:vec * KD + k + 1]), split)

            def empty(dst, func=ACT.Copy, **kw):
                b = pair_take()
                act.activation(dst, b[:, 0:dst.free_size()], func, **kw).then_inc(pair_free, 1)

            def take_gate_row():
                for half in range(2):
                    empty(gate_row[:, half * W:(half + 1) * W])

            def load_ln_rows(layer, sub):
                act.dma_start(g_row, ln_g[layer, sub, :].partition_broadcast(P)).then_inc(ln_rows, 16)
                act.dma_start(b_row, ln_b[layer, sub, :].partition_broadcast(P)).then_inc(ln_rows, 16)

            def deviation(stage, t):
                act.wait_ge(var_ready, NT * stage + t + 1)
                act.activation(stat[:, t, 14:15], stat[:, t, 13:14], ACT.Sqrt).then_inc(std_ready, 1)

            modulate(0, 0)
            splits.ahead(("qkv", 0), 2)
            act.wait_ge(angles_ready, 1)
            act.activation(ang[:, 2:4], ang[:, 2:4], ACT.Sin).then_inc(sincos_ready, 1)
            act.wait_ge(lb_logits_ready, 1)
            act.activation(lbc[:, 3:5, :], lbc[:, 0:2, :], ACT.Exp).then_inc(lb_exp_ready, 1)
            for u in range(4):
                splits.ahead(("qkv", u), 2)
                for t in range(NT):
                    empty(tok[:, t, u * W:(u + 1) * W])
            splits.ahead(("qkv", 4), 2)
            for t in range(NT):
                empty(tok[:, t, 4 * W:5 * W])
            splits.ahead(("qkv", 4))
            for j in range(4):
                empty(q_f[:, 2 * j:2 * j + 2, :].rearrange("p k s -> p (k s)"))
            load_ln_rows(0, 0)
            splits.ahead(("qkv", 5), 2)
            for t in range(NT):
                empty(tok[:, t, 5 * W:6 * W])
            splits.ahead(("qkv", 5))
            for j in range(4):
                empty(k_f[:, 2 * j:2 * j + 2, :].rearrange("p k s -> p (k s)"))
            take_gate_row()

            for h in range(NH + 2):
                if h < NH:
                    b = pair_take()
                    r = h % 2
                    act.wait_ge(row_max_ready, h + 1)
                    if h >= 2:
                        act.wait_ge(turn_full, h - 1)
                    act.activation(probs[:, r, 0:P], b[:, 0:P], ACT.Exp, bias=sm[:, r, 2:3], scale=SCALE,
                                   accum_out=sm[:, r, 4:5])
                    act.activation(probs[:, r, P:3 * P], b[:, P:3 * P], ACT.Exp, bias=sm[:, r, 3:4], scale=SCALE,
                                         accum_out=sm[:, r, 5:6]).then_inc(pair_free, 1)
                if h >= 2:
                    act.wait_ge(head_full, h - 1)
                    act.activation(l_hi[:, h - 2, :], Y_B[0][:, 0:SEQ], ACT.Copy).then_inc(head_hi, 1)
                if 1 <= h <= NH:
                    act.wait_ge(turn_full, h)
                    if h >= 3:
                        act.wait_ge(head_full, h - 2)
                    act.activation(probs_f[:, (h - 1) % 2, :], TURN_B[:, 0:3 * P], ACT.Copy).then_inc(turn_free, 1)
            splits.ahead(("wo", 1))
            modulate(0, 3, stage=0)

            act.wait_ge(x_ready, NT)
            load_ln_rows(0, 1)

            def silu(g, t):
                width = FGROUPS[g][1]
                act.wait_ge(gate_full, NT * g + t + 1)
                act.activation(h_t[:, t, 0:width], GATE_B[:, 0:width], ACT.Silu).then_inc(silu_ready, 1)

            def turned_hi(n, width, full, ready):
                act.wait_ge(full, n)
                act.activation(hf_hi[:, 0:width // P, :].rearrange("p k s -> p (k s)"), TURN_B[:, 0:width],
                               ACT.Copy).then_inc(ready, 1)

            for g in range(len(FGROUPS)):
                splits.ahead(("gate", g), 0)
                silu(g, 0)
                splits.ahead(("gate", g), 3)
                silu(g, 1)
                turned_hi(NT * g + 1, FGROUPS[g][1], hturn_full, hf_hi_ready)
                splits.ahead(("up", g), 4)
                turned_hi(NT * g + 2, FGROUPS[g][1], hturn_full, hf_hi_ready)
            splits.ahead(("down", len(FGROUPS) - 1), 2)
            take_gate_row()
            modulate(1, 0, stage=1)

            for u in range(8):
                splits.ahead(("rec", u), 2)
                if u == 4:
                    act.wait_ge(fgate_ready, 1)
                    act.activation(buf_c[:], buf_c[:], ACT.Ln).then_inc(logf_ready, 1)
                for t in range(NT):
                    i = NT * u + t
                    if u < 4:
                        if i >= 2:
                            act.wait_ge(recturn_full, i - 1)
                        empty(stage_rows[i % 2], ACT.Silu if u < 2 else ACT.Sigmoid)
                    elif u < 6:
                        empty(v_t[:, t, (u - 4) * W:(u - 3) * W])
                    else:
                        empty(y_t[:, t, (u - 6) * W:(u - 5) * W], ACT.Silu)
                if u == 4:
                    act.wait_ge(gcum_ready, 1)
                    act.activation(last[:, 1], last[:, 0], ACT.Exp).then_inc(expg_ready, 1)
                    act.activation(buf_c[:], buf_d[:], ACT.Exp).then_inc(expg_ready, 1)
                if u == 5:
                    act.wait_ge(expg_used, 1)
                    act.activation(buf_c[:], buf_d[:], ACT.Exp, scale=-1.0).then_inc(expng_ready, 1)
                if u == 6:
                    act.wait_ge(expng_ready, 1)
                    for h in range(NH):
                        for j in range(3):
                            cols = buf_d[:, h, j * CHUNK:(j + 1) * CHUNK]
                            act.activation(cols, cols, ACT.Exp, bias=last[:, 0, h, j:j + 1],
                                           scale=-1.0).then_inc(expst_ready, 1)
            splits.ahead(("rec", 7))
            for j in range(4):
                t, half = j // 2, j % 2
                empty(ks_t[:, t, half * W:(half + 1) * W])
            for h in range(NH):
                pair[0] += 1
                if h % 4 == 3:
                    for t in range(NT):
                        act.wait_ge(o_full, NT * h + t + 1)
                        sl = slice(h // 4 * W, (h // 4 + 1) * W)
                        act.activation(tok[:, t, sl], Y_B[2 * t + h // 4][:], ACT.Copy).then_inc(o_ready, 1)
            for t in range(NT):
                for half in range(2):
                    act.activation(tok[:, t, D + half * W:D + (half + 1) * W], Y_B[2 * t + half][:],
                                   ACT.Square).then_inc(sq_ready, 1)
            for t in range(NT):
                act.wait_ge(msq_ready, t + 1)
                act.activation(rms[:, t, 1, :], rms[:, t, 0, :], ACT.Sqrt).then_inc(rms_ready, 1)
            for t in range(NT):
                for half in range(2):
                    split_left(t, half, lambda k: dict(func=ACT.Copy, scale=normc[:, k:k + 1]))
            load_ln_rows(1, 0)
            act.dma_start(wr, router_w[0].rearrange("(k p) e -> p k e", p=P)).then_inc(wr_loaded, 16)
            splits.ahead(("rwo", 0))
            take_gate_row()
            splits.ahead(("rwo", 1))
            modulate(1, 3, split=False, stage=2)

            act.wait_ge(x_ready, 3 * NT)
            load_ln_rows(1, 1)
            for t in range(NT):
                act.wait_ge(gap_ready, t + 1)
                act.activation(rt[:, t, 5, 2:3], rt[:, t, 5, 0:1], ACT.Exp).then_inc(gap_exp, 1)

            take_gate_row()

            def experts(p):
                me = moe_sems[p]

                def gathered(count, half, buffer):
                    act.wait_ge(me["pick_full"], count)
                    for j in range(4):
                        k = 4 * half + j
                        ins = act.activation(temp_flat[:, k * P:(k + 1) * P], SMALL_B[:, j * P:(j + 1) * P],
                                             ACT.Identity, scale=modc[:, 1, 4 * KD + k:4 * KD + k + 1],
                                             bias=modc[:, 1, 3 * KD + k:3 * KD + k + 1])
                    ins.then_inc(me["ue_ready"], 1)
                    act.wait_ge(me["ue_ready"], count)
                    act.activation(ue_hi[:, buffer, 4 * half:4 * half + 4, :].rearrange("p k s -> p (k s)"),
                                   temp_flat[:, half * W:(half + 1) * W], ACT.Copy).then_inc(me["ue_hi_ready"], 1)

                gathered(1, 0, 0)
                for j in range(4):
                    empty(put_all[:, SEQ + j * W:SEQ + (j + 1) * W])
                gathered(2, 1, 0)
                splits.start_pass(p)

                def pair_of_experts(pr, final):
                    splits.start_pair(p, pr, final)
                    for r in range(2):
                        for g in range(EGROUPS):
                            step = r * EGROUPS + g
                            done = pr * (2 * EGROUPS) + step
                            splits.ahead_in_pair(r, ("gate", g))
                            act.wait_ge(me["gate_full"], done + 1)
                            act.activation(h_t[:, step % 2, :], GATE_B[:], ACT.Silu).then_inc(me["silu_ready"], 1)
                            if g >= 1:
                                turned_hi(done, W, me["hturn_full"], me["hf_hi_ready"])
                            if g in (2, 4):
                                half = g // 2 - 1
                                splits.ahead_in_pair(r, ("down", g - 1))
                                gathered(pr * 4 + (2 * r + 2 + half + 1), half, (r + 1) % 2)
                        splits.ahead_in_pair(r, ("down", EGROUPS - 2))
                        turned_hi(pr * (2 * EGROUPS) + (r + 1) * EGROUPS, W, me["hturn_full"], me["hf_hi_ready"])
                        splits.ahead_in_pair(r, ("down", EGROUPS - 1))
                        act.wait_ge(me["down_done"], pr * (2 * EGROUPS) + (r + 1) * EGROUPS)
                        for half in range(2):
                            act.activation(ye[:, half * W:(half + 1) * W], Y_B[half][:],
                                           ACT.Copy).then_inc(me["ye_ready"], 1)
                    splits.ahead_in_pair(1, ("down", EGROUPS - 1), SPLITS)

                act.sem_inc(me["ye_ready"], 1)
                with act.Fori(0, NE // 2 - 1) as pr:
                    pair_of_experts(pr, False)
                pair_of_experts(NE // 2 - 1, True)

            experts(0)
            act.wait_ge(flag_ready, 1)
            overflow = act.value_load(flag[0:1, 0:1], min_val=0, max_val=1)
            with act.If(overflow > 0):
                experts(1)
            for t in range(NT):
                deviation(3, t)
            for t in range(NT):
                act.wait_ge(x_ready, 3 * NT + t + 1)
                act.dma_start(out[0, t * P:(t + 1) * P, :], x_t[:, t, :]).then_inc(out_stored, 16)
            act.wait_ge(out_stored, 16 * NT)

        @block.tensor
        def _(pe):
            pair = [0]

            def claim():
                n, pair[0] = pair[0], pair[0] + 1
                return pair_claim(pe, n)

            def three_passes(dst, hi, lo, w_hi_k, w_lo_k, start, stop):
                pe.matmul(dst, hi, w_hi_k, start=start, stop=False)
                pe.matmul(dst, hi, w_lo_k, start=False, stop=False)
                return pe.matmul(dst, lo, w_hi_k, start=False, stop=stop)

            def chunks(m, k_n, n):
                return [w[:, m % SPLITS, 0:k_n * n].rearrange("p (k n) -> p k n", n=n) for w in (w_hi, w_lo)]

            LEFTS = [("qkv", 0), ("gate", 0), ("rec", 0), ("rwo", 0)]

            def wide_part(dst, hi, lo, t, m, h, n=W):
                whi, wlo = chunks(m, 4, n)
                for k in range(4):
                    kk, ts = 4 * h + k, slice(t * P, (t + 1) * P)
                    ins = three_passes(dst[:, 0:n], hi[:, kk, ts], lo[:, kk, ts], whi[:, k, :], wlo[:, k, :],
                                       start=(kk == 0), stop=(kk == KD - 1))
                return ins

            def product(dst, unit, t, n=W):
                if unit in LEFTS:
                    pe.wait_ge(l_lo_ready, 4 * LEFTS.index(unit) + 2 * t + 2)
                for h in range(2):
                    m = SPLIT_AT[unit, h]
                    if t == 0:
                        pe.wait_ge(raw_used, RAW_AT[unit, h] + 1)
                    ins = wide_part(dst, l_hi, l_lo, t, m, h, n)
                    if t == NT - 1 and h == 0:
                        ins.then_inc(firsts_used, 1)
                return ins

            def down_part(banks, k0, m, start, stop):
                whi, wlo = chunks(m, 2, D)
                for k in range(2):
                    for half in range(2):
                        hs = slice(half * W, (half + 1) * W)
                        ins = three_passes(banks[half][:], hf_hi[:, k0 + k, :], hf_lo[:, k0 + k, :],
                                           whi[:, k, hs], wlo[:, k, hs], start=(start and k == 0),
                                           stop=(stop and k == 1))
                return ins

            def turn_four(dst, ins_of):
                for j in range(4):
                    ins = pe.transpose(dst[:, j * P:(j + 1) * P], ins_of(j), ident[:])
                return ins

            def add_partitions(a):
                if a:
                    pe.wait_ge(ada_cols_read, a)
                pe.wait_ge(raw_used, RAW_AT[("ada", a), 1] + 1)
                for j in range(4):
                    ins = pe.matmul(SMALL_B[:, j:j + 1], acc[:, a % 2, j * P:(j + 1) * P], ones[:, 0:1],
                                    start=True, stop=True)
                ins.then_inc(ada_cols_full, 1)

            def turn_x(stage, tiles=range(NT)):
                for t in tiles:
                    if stage:
                        pe.wait_ge(x_ready, NT * (stage - 1) + t + 1)
                    for half in range(2):
                        turn_four(claim(), lambda j: x_t[:, t, (4 * half + j) * P:(4 * half + j + 1) * P])\
                            .then_inc(pair_full, 1)

            def turn_x_and_start(stage, unit):
                turn_x(stage, [0])
                pe.wait_ge(ada_cols_read, 10 if stage == 1 else ADA_IN_REC)
                turn_x(stage, [1])
                return product(PAIR[0], unit, 0)

            def gate_row_product(stage):
                pe.wait_ge(diag_ready, stage + 1)
                for half in range(2):
                    pe.matmul(claim()[:], ones[:], diags[stage][:, half * W:(half + 1) * W],
                              start=True, stop=True).then_inc(pair_full, 1)

            pe.wait_ge(consts_ready, 1)
            pe.wait_ge(smalls_loaded, 16 * 4)
            pe.transpose(SMALL_B[:, 0:KD], c_rows, ident[0:KD, 0:KD])
            nu = DEPTH * ADA_UNITS
            for j in range(4):
                pe.transpose(SMALL_B[:, 4 * KD + j * nu:4 * KD + (j + 1) * nu], ab_rows[:, j * P:(j + 1) * P],
                             ident[0:nu, 0:nu])
            pe.transpose(SMALL_B[:, KD:3 * KD], lb_rows, ident[0:2 * KD, 0:2 * KD])
            pe.transpose(SMALL_B[:, 3 * KD:4 * KD], nw_rows, ident[0:KD, 0:KD]).then_inc(rows_turned, 1)
            pe.wait_ge(x_loaded, 16)
            turn_x(0, [0])
            pe.wait_ge(c_ready, 1)
            pe.wait_ge(rows_read, 1)
            for a in range(4):
                add_partitions(a)
            turn_x(0, [1])

            def project_qkv(u):
                for t in range(NT):
                    product(claim(), ("qkv", u), t).then_inc(pair_full, 1)

            for u in range(5):
                project_qkv(u)
                if u >= 1:
                    add_partitions(3 + u)
            pe.wait_ge(rotated, NT)

            def turn_heads(first_column):
                for j in range(4):
                    turn_four(claim(), lambda i: tok[:, i % 2, first_column + (2 * j + i // 2) * P:
                                                     first_column + (2 * j + i // 2 + 1) * P]).then_inc(pair_full, 1)

            turn_heads(0)
            project_qkv(5)
            add_partitions(8)
            turn_heads(D)
            add_partitions(9)
            gate_row_product(0)
            pe.wait_ge(pair_free, PAIR_AT["gate_row0"])
            for i in range(NH + 2):
                if i < NH:
                    b = claim()
                    pe.matmul(b[:, 0:P], q_f[:, i, 0:P], k_f[:, i, 0:P], start=True, stop=True)
                    pe.matmul(b[:, P:3 * P], q_f[:, i, P:SEQ], k_f[:, i, :], start=True, stop=True).then_inc(pair_full, 1)
                if i >= 2:
                    h = i - 2
                    pe.wait_ge(turn_free, h + 1)
                    if h:
                        pe.wait_ge(head_free, h)
                    pe.matmul(Y_B[0][:, 0:SEQ], v_t[:, 0, h * P:(h + 1) * P], probs_f[:, h % 2, 0:SEQ],
                              start=True, stop=False)
                    pe.matmul(Y_B[0][:, P:SEQ], v_t[:, 1, h * P:(h + 1) * P], probs_f[:, h % 2, SEQ:SEQ + P],
                              start=False, stop=True).then_inc(head_full, 1)
                if 1 <= i <= NH:
                    h = i - 1
                    pe.wait_ge(probs_ready, h + 1)
                    if h:
                        pe.wait_ge(turn_free, h)
                    for j in range(3):
                        ins = pe.transpose(TURN_B[:, j * P:(j + 1) * P], probs[:, h % 2, j * P:(j + 1) * P], ident[:])
                    ins.then_inc(turn_full, 1)
            pe.wait_ge(head_free, NH)
            for u in range(2):
                for t in range(NT):
                    product(Y_B[2 * t + u], ("wo", u), t).then_inc(y_full, 1)

            turn_x_and_start(1, ("gate", 0)).then_inc(gate_full, 1)
            pe.wait_ge(pair_free, PAIR_AT["gate_row1"])
            steps = len(FGROUPS) * NT

            def turn_h(g, t):
                pe.wait_ge(h_ready, NT * g + t + 1)
                if NT * g + t:
                    pe.wait_ge(hf_ready, NT * g + t)
                for j in range(FGROUPS[g][1] // P):
                    ins = pe.transpose(TURN_B[:, j * P:(j + 1) * P], h_t[:, t, j * P:(j + 1) * P], ident[:])
                ins.then_inc(hturn_full, 1)

            def down(g, t):
                pe.wait_ge(hf_ready, NT * g + t + 1)
                n = parts_of(("down", g))
                for h in range(n):
                    m = SPLIT_AT[("down", g), h]
                    if t == 0:
                        pe.wait_ge(raw_used, RAW_AT[("down", g), h] + 1)
                    if g == 0 and h == 0:
                        pe.wait_ge(y_read, NT)
                    ins = down_part(Y_B[2 * t:2 * t + 2], 2 * h, m, g == 0 and h == 0,
                                    g == len(FGROUPS) - 1 and h == n - 1)
                    if t == NT - 1 and h < n - 1:
                        ins.then_inc(firsts_used, 1)
                ins.then_inc(down_done, 1)

            for g in range(len(FGROUPS)):
                width = FGROUPS[g][1]
                if g:
                    pe.wait_ge(silu_ready, NT * g)
                    product(GATE_B, ("gate", g), 0, width).then_inc(gate_full, 1)
                    down(g - 1, 1)
                    add_partitions(10 + 2 * g)
                pe.wait_ge(silu_ready, NT * g + 1)
                product(GATE_B, ("gate", g), 1, width).then_inc(gate_full, 1)
                if g == 0:
                    add_partitions(10)
                product(UP_B, ("up", g), 0, width).then_inc(up_full, 1)
                add_partitions(11 + 2 * g)
                turn_h(g, 0)
                product(UP_B, ("up", g), 1, width).then_inc(up_full, 1)
                down(g, 0)
                turn_h(g, 1)
            pe.wait_ge(silu_ready, steps)
            gate_row_product(1)
            down(len(FGROUPS) - 1, 1)

            turn_x_and_start(2, ("rec", 0)).then_inc(pair_full, 1)
            pair[0] += 1

            def turn_stage(i):
                pe.wait_ge(pair_free, PAIR_AT["rec"] + i + 1)
                if i:
                    pe.wait_ge(recturn_read, i)
                turn_four(TURN_B, lambda j: stage_rows[i % 2][:, j * P:(j + 1) * P]).then_inc(recturn_full, 1)

            for u in range(8):
                for t in range(NT):
                    i = NT * u + t
                    if i:
                        product(claim(), ("rec", u), t).then_inc(pair_full, 1)
                    if 1 <= i <= 4 * NT:
                        turn_stage(i - 1)
                if u < 2:
                    add_partitions(ADA_IN_REC + u)
            pe.wait_ge(decs_ready, 3)
            for j in range(4):
                t, half = j // 2, j % 2
                turn_four(claim(), lambda i: buf_b[:, 4 * half + i, t * P:(t + 1) * P]).then_inc(pair_full, 1)
            pe.wait_ge(pair_free, PAIR_AT["intra"])
            pe.wait_ge(y_read, 2 * NT)
            for i in range(NH + 1):
                if i < NH:
                    h = i
                    b = claim()
                    for t in range(NT):
                        ts = slice(t * P, (t + 1) * P)
                        ins = pe.matmul(b[:, ts], buf_c[:, h, ts], big_a[:, h, ts], start=True, stop=True)
                    ins.then_inc(pair_full, 1)
                    if h:
                        pe.wait_ge(states_ready, h)
                    for j in range(3):
                        rows = slice(j % 2 * CHUNK, (j % 2 + 1) * CHUNK)
                        ins = pe.matmul(kv_products[j], ks_t[rows, j // 2, h * P:(h + 1) * P],
                                        v_t[rows, j // 2, h * P:(h + 1) * P], start=True, stop=True)
                    ins.then_inc(kv_full, 1)
                if i >= 1:
                    h = i - 1
                    pe.wait_ge(pair_free, PAIR_AT["intra"] + h + 1)
                    pe.wait_ge(states_ready, h + 1)
                    hs = slice(h % 4 * P, (h % 4 + 1) * P)
                    for t in range(NT):
                        b = Y_B[2 * t + h // 4]
                        for ch in range(2 * t, 2 * t + 2):
                            rows = slice(ch % 2 * CHUNK, (ch % 2 + 1) * CHUNK)
                            ins = pe.matmul(b[rows, hs], intra[:, h % 2, ch * CHUNK:(ch + 1) * CHUNK],
                                            v_t[:, t, h * P:(h + 1) * P], start=True, stop=(ch == 0))
                            if ch:
                                ins = pe.matmul(b[rows, hs], big_a[:, h, ch * CHUNK:(ch + 1) * CHUNK],
                                                states[:, h % 2, ch - 1, :], start=False, stop=True)
                        ins.then_inc(o_full, 1)
            for t in range(NT):
                pe.wait_ge(o_gated, t + 1)
                for half in range(2):
                    turn_four(claim(), lambda j: tok[:, t, (4 * half + j) * P:(4 * half + j + 1) * P])\
                        .then_inc(pair_full, 1)
            pe.wait_ge(sq_ready, 2 * NT)
            for u in range(2):
                for t in range(NT):
                    product(Y_B[2 * t + u], ("rwo", u), t).then_inc(y_full, 1)
                if u == 0:
                    gate_row_product(2)

            pe.wait_ge(wr_loaded, 16)
            for t in range(NT):
                turn_x(3, [t])
                pe.wait_ge(pair_free, PAIR_AT["mod3"] + 2 * (t + 1))
                for k in range(KD):
                    ins = pe.matmul(TURN_B[:, t * NE:(t + 1) * NE], big_a[:, k, t * P:(t + 1) * P], wr[:, k, :],
                                    start=(k == 0), stop=(k == KD - 1))
            ins.then_inc(logits_full, 1)
            gate_row_product(3)
            pe.wait_ge(masks_ready, 1)
            mask = [rt[:, t, 6, :] for t in range(NT)]
            pe.matmul(SMALL_B[:, 0:NE], before[:], mask[0], start=True, stop=True)
            pe.matmul(SMALL_B[:, NE:2 * NE], before[:], mask[1], start=True, stop=False)
            pe.matmul(SMALL_B[:, NE:2 * NE], ones[:], mask[0], start=False, stop=True)
            pe.matmul(SMALL_B[:, 2 * NE:3 * NE], ones[:], mask[0], start=True, stop=False)
            pe.matmul(SMALL_B[:, 2 * NE:3 * NE], ones[:], mask[1], start=False, stop=True).then_inc(places_full, 1)

            def experts(p):
                me = moe_sems[p]

                def gather(e, half):
                    for j in range(4):
                        k = 4 * half + j
                        for t in range(NT):
                            ins = pe.matmul(SMALL_B[:, j * P:(j + 1) * P], x_t[:, t, k * P:(k + 1) * P],
                                            pick[:, bass.ds(e * SEQ + t * P, P)], start=(t == 0), stop=(t == NT - 1))
                    ins.then_inc(me["pick_full"], 1)

                def scatter(event):
                    pe.wait_ge(me["put_ready"], event + 1)
                    for n in range(4):
                        t, half = n // 2, n % 2
                        if n >= 2:
                            pe.wait_ge(me["put_added"], event * 4 + (n - 1))
                        pe.matmul(Y_B[2 + n % 2][:], put[:, t * P:(t + 1) * P], ye[:, half * W:(half + 1) * W],
                                  start=True, stop=True).then_inc(me["put_full"], 1)

                def turn_h(steps_done, step):
                    pe.wait_ge(me["h_ready"], steps_done)
                    turn_four(TURN_B, lambda j: h_t[:, step % 2, j * P:(j + 1) * P]).then_inc(me["hturn_full"], 1)

                pe.wait_ge(me["picks_ready"], 1)
                gather(0, 0)
                pe.wait_ge(me["picks_ready"], 2)
                for j in range(4):
                    turn_four(claim(), lambda i: put_raw[:, j // 2, 2 * (j % 2) + i // 2,
                                                         i % 2 * P:(i % 2 + 1) * P]).then_inc(pair_full, 1)
                pe.wait_ge(me["ue_ready"], 1)
                gather(0, 1)
                pe.wait_ge(pair_free, PAIR_AT["turn_put"] + 4 * (p + 1))
                pe.wait_ge(me["picks_ready"], 3)
                pe.wait_ge(zeros_ready, 1)
                with pe.Fori(0, NE // 2) as pr:
                    for r in range(2):
                        def part_of(kind, g, h):
                            i = r * PARTS_PER_EXPERT + EXPERT_END[kind, g] - 1 + h
                            pe.wait_ge(raw_used, pr * PARTS_PER_PAIR + (raw_index(p, i) + 1))
                            return split_index(p, i)

                        def expert_product(dst, kind, g):
                            for h in range(2):
                                m = part_of(kind, g, h)
                                ins = wide_part(dst, ue_hi[:, r], ue_lo[:, r], 0, m, h)
                                if h == 0:
                                    ins.then_inc(firsts_used, 1)
                            return ins

                        def down(g):
                            pe.wait_ge(me["hf_ready"], pr * (2 * EGROUPS) + (r * EGROUPS + g + 1))
                            if g == 0:
                                pe.wait_ge(me["ye_ready"], pr * 4 + (2 * r + 1))
                            for h in range(2):
                                m = part_of("down", g, h)
                                ins = down_part(Y_B[0:2], 2 * h, m, g == 0 and h == 0, g == EGROUPS - 1 and h == 1)
                                if h == 0:
                                    ins.then_inc(firsts_used, 1)
                            ins.then_inc(me["down_done"], 1)

                        pe.wait_ge(me["ue_split"], pr * 4 + 2 * (r + 1))
                        for g in range(EGROUPS):
                            done = pr * (2 * EGROUPS) + (r * EGROUPS + g)
                            if g >= 1:
                                pe.wait_ge(me["silu_ready"], done)
                            expert_product(GATE_B, "gate", g).then_inc(me["gate_full"], 1)
                            if g >= 1:
                                turn_h(done, r * EGROUPS + g - 1)
                            expert_product(UP_B, "up", g).then_inc(me["up_full"], 1)
                            if g >= 1:
                                down(g - 1)
                            if g in (2, 4):
                                half = g // 2 - 1
                                pe.wait_ge(me["ue_ready"], pr * 4 + (2 * r + 2 + half))
                                gather(pr * 2 + (r + 1), half)
                        turn_h(pr * (2 * EGROUPS) + (r + 1) * EGROUPS, (r + 1) * EGROUPS - 1)
                        scatter(pr * 2 + r)
                        down(EGROUPS - 1)
                pe.wait_ge(me["ye_ready"], 2 * NE + 1)
                scatter(NE)

            experts(0)
            pe.wait_ge(flag_ready, 1)
            overflow = pe.value_load(flag[0:1, 0:1], min_val=0, max_val=1)
            with pe.If(overflow > 0):
                experts(1)

        @block.vector
        def _(dve):
            n = [0]

            def step(ins):
                n[0] += 1
                ins.then_inc(dve_step, 1)

            def settled():
                dve.wait_ge(dve_step, n[0])

            dve.wait_ge(rows_turned, 1)
            dve.wait_ge(c_ready, 1)
            step(dve.tensor_copy(lbc[:, 0:2, :].rearrange("p l k -> p (l k)"), SMALL_B[:, KD:3 * KD]))
            step(dve.tensor_copy(bias_c[:].rearrange("p j a -> p (j a)"),
                                 SMALL_B[:, 4 * KD:4 * KD + 4 * DEPTH * ADA_UNITS]))
            dve.tensor_copy(normc[:], SMALL_B[:, 3 * KD:4 * KD]).then_inc(rows_read, 1)
            settled()
            plus_one = bias_c[:].rearrange("p j (l v h) -> p (j l) v h", l=DEPTH, h=2)
            for vec in (1, 2, 4, 5):
                step(dve.tensor_scalar(plus_one[:, :, vec, :], plus_one[:, :, vec, :], 1.0, None, ALU.add))
            settled()

            def low_part(m, raw_i, hi_count, n):
                dve.wait_ge(hi_ready, hi_count)
                dve.tensor_tensor(w_lo[:, m % SPLITS, 0:n], raw[:, raw_i % SLOTS, 0:n],
                                  w_hi[:, m % SPLITS, 0:n].bitcast(F32), ALU.subtract).then_inc(raw_used, 1)

            def ada_part(a, h):
                i = RAW_AT[("ada", a), h]
                dve.wait_ge(raw_filled[i % SLOTS], 16 * (i // SLOTS + 1))
                if h == 1 and a not in (0, 4, 10, ADA_IN_REC):
                    ada_read(a - 1)
                w = raw[:, i % SLOTS, :].rearrange("p (k n) -> p k n", n=W)
                dst = acc[:, a % 2, :]
                for k in range(4):
                    kk = 4 * h + k
                    if kk == 0:
                        ins = dve.tensor_scalar(dst, w[:, k, :], ccol[:, kk:kk + 1], None, ALU.mult)
                    else:
                        if k == 0:
                            dve.wait_ge(raw_used, i)
                        else:
                            settled()
                        ins = dve.scalar_tensor_tensor(out=dst, in0=w[:, k, :], scalar=ccol[:, kk:kk + 1], in1=dst,
                                                       op0=ALU.mult, op1=ALU.add)
                    if k < 3:
                        step(ins)
                ins.then_inc(raw_used, 1)

            def ada_read(a):
                layer, vec, half = a // ADA_UNITS, a % ADA_UNITS // 2, a % 2
                dve.wait_ge(ada_cols_full, a + 1)
                dve.tensor_tensor(modc[:, layer, vec * KD + 4 * half:vec * KD + 4 * half + 4], SMALL_B[:, 0:4],
                                  bias_c[:, :, a], ALU.add).then_inc(ada_cols_read, 1)

            def before_experts(m):
                i = RAW_AT[SPLIT[m]]
                first = i
                while first > 8 and RAW[first - 1][0][0] == "ada":
                    first -= 1
                for j in range(first, i):
                    ada_part(RAW[j][0][1], RAW[j][1])
                low_part(m, i, m + 1, raw_source(*SPLIT[m])[1])

            def expert_part(p, pr, i):
                n, m = raw_index(p, i), split_index(p, i)
                low_part(m, n, pr * PARTS_PER_PAIR + (m + 1), PART)

            splits = Splits(before_experts, expert_part)

            def left_low(t, half, count):
                dve.wait_ge(l_hi_ready, count)
                ks, ts = slice(4 * half, 4 * half + 4), slice(t * P, (t + 1) * P)
                dve.tensor_tensor(l_lo[:, ks, ts], big_a[:, ks, ts], l_hi[:, ks, ts].bitcast(F32), ALU.subtract)\
                   .then_inc(l_lo_ready, 1)

            def left_lows(first, tiles=range(NT)):
                for t in tiles:
                    for half in range(2):
                        left_low(t, half, first + 2 * t + half + 1)

            def make_diag(stage):
                layer, vec = stage // 2, 2 + 3 * (stage % 2)
                dve.wait_ge(ada_cols_read, layer * ADA_UNITS + 2 * vec + 2)
                for k in range(KD):
                    ins = dve.tensor_scalar(diags[stage][:, k * P:(k + 1) * P], ident[:],
                                            modc[:, layer, vec * KD + k:vec * KD + k + 1], None, ALU.mult)
                ins.then_inc(diag_ready, 1)

            def norm(stage):
                if stage < 2:
                    dve.wait_ge(raw_used, RAW_AT[("ada", ADA_IN_REC - 1 if stage else 9), 1] + 1)
                dve.wait_ge(pair_free, PAIR_AT[f"gate_row{stage}"] + 2)
                dve.wait_ge(ln_rows, 32 * (stage + 1))
                for t in range(NT):
                    st = stat[:, t, :]
                    if stage == 0 or stage == 2:
                        dve.wait_ge(y_full, 2 * stage + 3 + t)
                    if stage == 1:
                        dve.wait_ge(down_done, len(FGROUPS) * NT - 1 + t)
                    for half in range(2):
                        hs = slice(half * W, (half + 1) * W)
                        y = y_t[:, t, hs] if stage == 3 else Y_B[2 * t + half][:]
                        ins = dve.tensor_tensor(y_t[:, t, hs], y, gate_row[:, hs], ALU.mult)
                        if half == 0 or stage == 3:
                            step(ins)
                        else:
                            ins.then_inc(y_read, 1)
                    settled()
                    if stage < 3:
                        dve.wait_ge(y_read, NT * stage + t + 1)
                    step(dve.scalar_tensor_tensor(out=y_t[:, t, :], in0=x_t[:, t, :], scalar=ALPHA, in1=y_t[:, t, :],
                                                  op0=ALU.mult, op1=ALU.add))
                    settled()
                    for half in range(2):
                        step(dve.bn_stats(st[:, 6 * half:6 * half + 6], y_t[:, t, half * W:(half + 1) * W]))
                    settled()
                    step(dve.bn_aggr(st[:, 12:14], st[:, 0:12]))
                    settled()
                    dve.tensor_scalar(st[:, 13:14], st[:, 13:14], LN_EPS, None, ALU.add).then_inc(var_ready, 1)
                    step(dve.scalar_tensor_tensor(out=y_t[:, t, :], in0=y_t[:, t, :], scalar=st[:, 12:13], in1=g_row,
                                                  op0=ALU.subtract, op1=ALU.mult))
                    if t == 1 and stage < 2:
                        left_lows(4 * (stage + 1), [0])
                    dve.wait_ge(std_ready, NT * stage + t + 1)
                    step(dve.reciprocal(st[:, 15:16], st[:, 14:15]))
                    settled()
                    dve.scalar_tensor_tensor(out=x_t[:, t, :], in0=y_t[:, t, :], scalar=st[:, 15:16], in1=b_row,
                                             op0=ALU.mult, op1=ALU.add).then_inc(x_ready, 1)

            dve.wait_ge(consts_ready, 1)
            for a in range(4):
                for h in range(2):
                    ada_part(a, h)
            ada_read(3)
            left_lows(0)

            splits.ahead(("qkv", 0), 2)
            dve.wait_ge(pos_loaded, 16)
            step(dve.tensor_copy(pos_f[:], pos_i[:]))
            settled()
            for t in range(NT):
                step(dve.tensor_scalar(ang[:, 0, t, :], invf[:], pos_f[:, t:t + 1], None, ALU.mult))
            settled()
            step(dve.tensor_scalar(ang[:, 2], ang[:, 0], 1.0 / TWO_PI, None, ALU.mult))
            step(dve.tensor_scalar(ang[:, 3], ang[:, 0], 1.0 / TWO_PI, 0.25, ALU.mult, ALU.add))
            settled()
            step(dve.tensor_scalar(ang[:, 2:4], ang[:, 2:4], ROUND, None, ALU.add))
            settled()
            step(dve.tensor_scalar(ang[:, 2:4], ang[:, 2:4], ROUND, None, ALU.subtract))
            settled()
            step(dve.tensor_copy(ang[:, 1], ang[:, 0]))
            settled()
            for part in (PI_1, PI_2, PI_3):
                step(dve.scalar_tensor_tensor(out=ang[:, 0:2].rearrange("p a t j -> p (a t j)"),
                                              in0=ang[:, 2:4].rearrange("p a t j -> p (a t j)"), scalar=-part,
                                              in1=ang[:, 0:2].rearrange("p a t j -> p (a t j)"),
                                              op0=ALU.mult, op1=ALU.add))
                settled()
            step(dve.tensor_scalar(ang[:, 1], ang[:, 1], float(np.pi / 2), None, ALU.add))
            settled()
            dve.tensor_scalar(ang[:, 2:4], ang[:, 0:2], PI_F, -PI_F, ALU.min, ALU.max).then_inc(angles_ready, 1)
            l0, l1, m, e0, e1, total, inv, both = (lbc[:, i, :] for i in range(8))
            step(dve.tensor_tensor(m, l0, l1, ALU.max))
            settled()
            step(dve.tensor_tensor(l0, l0, m, ALU.subtract))
            dve.tensor_tensor(l1, l1, m, ALU.subtract).then_inc(lb_logits_ready, 1)
            splits.ahead(("qkv", 1), 2)
            dve.wait_ge(lb_exp_ready, 1)
            step(dve.tensor_tensor(total, e0, e1, ALU.add))
            settled()
            step(dve.reciprocal(inv, total))
            settled()
            step(dve.tensor_tensor(e0, e0, inv, ALU.mult))
            step(dve.tensor_tensor(e1, e1, inv, ALU.mult))
            settled()
            step(dve.tensor_tensor(both, e0, e1, ALU.add))
            settled()
            lb, one_less = l0, l1
            step(dve.tensor_tensor(lb, both, e0, ALU.subtract))
            settled()
            step(dve.tensor_scalar(one_less, lb, -1.0, 1.0, ALU.mult, ALU.add))
            splits.ahead(("qkv", 3), 3)

            dve.wait_ge(sincos_ready, 1)
            dve.wait_ge(pair_free, PAIR_AT["qk"] + 8)
            for t in range(NT):
                heads = tok[:, t, 0:2 * D].rearrange("p (h d) -> p h d", d=HD)
                t1, t2 = heads[:, :, 0:HALF], heads[:, :, HALF:ROPE]
                sin = ang[:, 2, t, :].unsqueeze(1).to_broadcast([P, 2 * NH, HALF])
                cos = ang[:, 3, t, :].unsqueeze(1).to_broadcast([P, 2 * NH, HALF])
                tmp = [arena[:, 1, (4 * t + i) * 256:(4 * t + i + 1) * 256].rearrange("p (h j) -> p h j", j=HALF)
                       for i in range(4)]
                for i, (a, b) in enumerate(((t1, cos), (t2, sin), (t2, cos), (t1, sin))):
                    step(dve.tensor_tensor(tmp[i], a, b, ALU.mult))
                settled()
                step(dve.tensor_tensor(t1, tmp[0], tmp[1], ALU.subtract))
                dve.tensor_tensor(t2, tmp[2], tmp[3], ALU.add).then_inc(rotated, 1)
            make_diag(0)
            splits.ahead(("qkv", 5), 1)
            ada_read(9)

            for i in range(NH + 2):
                if i < NH:
                    r = i % 2
                    dve.wait_ge(pair_full, PAIR_AT["scores"] + i + 1)
                    b = PAIR[(PAIR_AT["scores"] + i) % 2]
                    for col in (0, 2 * P):
                        step(dve.copy_predicated(b[:, col:col + P], future[:], neg[:, 0:1].to_broadcast([P, P])))
                    settled()
                    step(dve.tensor_reduce(sm[:, r, 0:1], b[:, 0:P], AX.X, ALU.max))
                    step(dve.tensor_reduce(sm[:, r, 1:2], b[:, P:3 * P], AX.X, ALU.max))
                    settled()
                    dve.tensor_scalar(sm[:, r, 2:4], sm[:, r, 0:2], -SCALE, None, ALU.mult).then_inc(row_max_ready, 1)
                if 1 <= i <= NH:
                    h, r = i - 1, (i - 1) % 2
                    dve.wait_ge(pair_free, PAIR_AT["scores"] + h + 1)
                    step(dve.reciprocal(sm[:, r, 6:8], sm[:, r, 4:6]))
                    settled()
                    step(dve.tensor_scalar(probs[:, r, 0:P], probs[:, r, 0:P], sm[:, r, 6:7], None, ALU.mult))
                    dve.tensor_scalar(probs[:, r, P:3 * P], probs[:, r, P:3 * P], sm[:, r, 7:8], None, ALU.mult)\
                       .then_inc(probs_ready, 1)
                if i >= 2:
                    dve.wait_ge(head_hi, i - 1)
                    dve.tensor_tensor(l_lo[:, i - 2, :], Y_B[0][:, 0:SEQ], l_hi[:, i - 2, :].bitcast(F32),
                                      ALU.subtract).then_inc(head_free, 1)
            splits.ahead(("wo", 1), 2)
            norm(0)
            left_lows(4, [1])

            def make_h(g, t):
                width = FGROUPS[g][1]
                dve.wait_ge(silu_ready, NT * g + t + 1)
                dve.wait_ge(up_full, NT * g + t + 1)
                dve.tensor_tensor(h_t[:, t, 0:width], h_t[:, t, 0:width], UP_B[:, 0:width], ALU.mult)\
                   .then_inc(h_ready, 1)

            def turned_low(n, width, hi, ready):
                dve.wait_ge(hi, n)
                dve.tensor_tensor(hf_lo[:, 0:width // P, :].rearrange("p k s -> p (k s)"), TURN_B[:, 0:width],
                                  hf_hi[:, 0:width // P, :].rearrange("p k s -> p (k s)").bitcast(F32),
                                  ALU.subtract).then_inc(ready, 1)

            for g in range(len(FGROUPS)):
                width = FGROUPS[g][1]
                splits.ahead(("up", g), 1)
                make_h(g, 0)
                turned_low(NT * g + 1, width, hf_hi_ready, hf_ready)
                if g < len(FGROUPS) - 1:
                    splits.ahead(("down", g), 1)
                make_h(g, 1)
                if g < len(FGROUPS) - 1:
                    splits.ahead(("down", g), 2)
                turned_low(NT * g + 2, width, hf_hi_ready, hf_ready)
                if g == 1:
                    make_diag(1)
            ada_read(ADA_IN_REC - 1)
            norm(1)
            splits.ahead(("down", len(FGROUPS) - 1), 2)
            left_lows(8, [1])

            for i in range(4 * NT):
                u, t = i // NT, i % NT
                splits.ahead(("rec", u), 2)
                dve.wait_ge(recturn_full, i + 1)
                dst = (big_a if u < 2 else buf_b)[:, u % 2 * 4:u % 2 * 4 + 4, t * P:(t + 1) * P]
                dve.tensor_copy(dst, TURN_B[:].rearrange("p (k s) -> p k s", k=4)).then_inc(recturn_read, 1)
                if i == 2 * NT:
                    ada_read(DEPTH * ADA_UNITS - 1)
            dve.wait_ge(recturn_read, 4 * NT)
            for k in range(KD):
                step(dve.tensor_scalar(buf_c[:, k, :], buf_b[:, k, :], one_less[:, k:k + 1], lb[:, k:k + 1],
                                       ALU.mult, ALU.add))
            settled()
            dve.tensor_scalar(buf_b[:], buf_c[:], -1.0, 1.0, ALU.mult, ALU.add).then_inc(fgate_ready, 1)
            splits.ahead(("rec", 4), 2)
            dve.wait_ge(logf_ready, 1)
            for h in range(NH):
                step(dve.tensor_tensor_scan(buf_d[:, h, :], carry[:], buf_c[:, h, :], 0.0, ALU.mult, ALU.add))
            settled()
            dve.tensor_copy(last[:, 0], buf_d[:].rearrange("p h (j c) -> p h j c", c=CHUNK)[:, :, :, CHUNK - 1])\
               .then_inc(gcum_ready, 1)
            dve.wait_ge(expg_ready, 2)
            dve.tensor_tensor(big_a[:], big_a[:], buf_c[:], ALU.mult).then_inc(expg_used, 1)
            splits.ahead(("rec", 5), 2)
            dve.wait_ge(expng_ready, 1)
            dve.tensor_tensor(buf_c[:], buf_b[:], buf_c[:], ALU.mult).then_inc(decs_ready, 1)
            splits.ahead(("rec", 6), 2)
            dve.wait_ge(expst_ready, 3 * NH)
            dve.wait_ge(decs_ready, 1)
            dve.tensor_tensor(buf_b[:, :, 0:3 * CHUNK], buf_b[:, :, 0:3 * CHUNK], buf_d[:, :, 0:3 * CHUNK], ALU.mult)\
               .then_inc(decs_ready, 1)
            dve.wait_ge(decs_ready, 2)
            dve.memset(intra, 0.0).then_inc(decs_ready, 1)
            splits.ahead(("rec", 7))
            dve.wait_ge(decs_ready, 3)
            for h in range(NH):
                r = h % 2
                if h >= 2:
                    dve.wait_ge(o_full, NT * (h - 1))
                dve.wait_ge(pair_full, PAIR_AT["intra"] + h + 1)
                dve.copy_predicated(intra[:, r, :], keep[:].rearrange("p t c -> p (t c)"),
                                    PAIR[(PAIR_AT["intra"] + h) % 2][:, 0:SEQ]).then_inc(pair_free, 1)
                dve.wait_ge(kv_full, h + 1)
                step(dve.tensor_copy(states[:, r, 0, :], kv_products[0]))
                for j in (1, 2):
                    settled()
                    ins = dve.scalar_tensor_tensor(out=states[:, r, j, :], in0=states[:, r, j - 1, :],
                                                   scalar=last[:, 1, h, j:j + 1], in1=kv_products[j],
                                                   op0=ALU.mult, op1=ALU.add)
                    if j == 1:
                        step(ins)
                ins.then_inc(states_ready, 1)
            dve.wait_ge(o_ready, 2 * NT)
            for t in range(NT):
                dve.wait_ge(sq_ready, 2 * (t + 1))
                step(dve.tensor_reduce(rms[:, t, 0, :], tok[:, t, D:2 * D].rearrange("p (h d) -> p h d", d=HD),
                                       AX.X, ALU.add))
                settled()
                dve.tensor_scalar(rms[:, t, 0, :], rms[:, t, 0, :], 1.0 / HD, RMS_EPS, ALU.mult, ALU.add)\
                   .then_inc(msq_ready, 1)
            for t in range(NT):
                dve.wait_ge(rms_ready, t + 1)
                step(dve.reciprocal(rms[:, t, 0, :], rms[:, t, 1, :]))
                settled()
                heads = tok[:, t, 0:D].rearrange("p (h d) -> p h d", d=HD)
                step(dve.tensor_tensor(heads, heads, rms[:, t, 0, :].unsqueeze(2).to_broadcast([P, NH, HD]), ALU.mult))
                settled()
                dve.tensor_tensor(tok[:, t, 0:D], tok[:, t, 0:D], y_t[:, t, :], ALU.mult).then_inc(o_gated, 1)
            left_lows(12)
            dve.wait_ge(o_gated, NT)
            make_diag(2)
            splits.ahead(("rwo", 1), 2)
            norm(2)

            make_diag(3)
            dve.wait_ge(x_ready, 3 * NT)
            step(dve.memset(y_t[:], 0.0))
            step(dve.memset(pick[:, NE * SEQ:(NE + 1) * SEQ], 0.0))
            step(dve.memset(put_all[:, 0:SEQ], 0.0))
            dve.memset(ye, 0.0).then_inc(zeros_ready, 1)
            splits.ahead(("rwo", 1))
            dve.wait_ge(logits_full, 1)
            dve.wait_ge(iota_ready, 1)
            step(dve.tensor_copy(rt[:, :, 0, :], TURN_B[:, 0:NT * NE].rearrange("p (t e) -> p t e", t=NT)))
            settled()
            for t in range(NT):
                logit, top, idx, first, second, w, mask, comb = (rt[:, t, i, :] for i in range(8))
                step(dve.max(top, logit))
                settled()
                step(dve.max_index(ridx[:, t, :], top, logit))
                dve.tensor_tensor(w[:, 0:1], top[:, 1:2], top[:, 0:1], ALU.subtract).then_inc(gap_ready, 1)
                settled()
                step(dve.tensor_copy(idx[:, 0:2], ridx[:, t, 0:2]))
                settled()
                step(dve.tensor_scalar(first, iota[:, 0:NE], idx[:, 0:1], None, ALU.is_equal))
                step(dve.tensor_scalar(second, iota[:, 0:NE], idx[:, 1:2], None, ALU.is_equal))
                dve.wait_ge(gap_exp, t + 1)
                step(dve.tensor_scalar(w[:, 3:4], w[:, 2:3], 1.0, None, ALU.add))
                settled()
                step(dve.reciprocal(w[:, 4:5], w[:, 3:4]))
                settled()
                step(dve.tensor_tensor(w[:, 5:6], w[:, 2:3], w[:, 4:5], ALU.mult))
                step(dve.tensor_scalar(comb, first, w[:, 4:5], None, ALU.mult))
                settled()
                step(dve.scalar_tensor_tensor(out=comb, in0=second, scalar=w[:, 5:6], in1=comb,
                                              op0=ALU.mult, op1=ALU.add))
                ins = dve.tensor_tensor(mask, first, second, ALU.add)
                if t < NT - 1:
                    step(ins)
            ins.then_inc(masks_ready, 1)
            settled()
            dve.wait_ge(places_full, 1)
            step(dve.tensor_copy(rt[:, :, 0, :], SMALL_B[:, 0:NT * NE].rearrange("p (t e) -> p t e", t=NT)))
            step(dve.tensor_reduce(over[:, 0:1], SMALL_B[:, NT * NE:(NT + 1) * NE], AX.X, ALU.max))
            settled()
            dve.tensor_scalar(flag, over[:, 0:1], float(CAP), None, ALU.is_gt).then_inc(flag_ready, 1)

            def experts(p):
                me = moe_sems[p]
                slots = iota[:, p * CAP:(p + 1) * CAP]

                def pick_tokens(experts):
                    for e in experts:
                        for t in range(NT):
                            ins = dve.tensor_scalar(pick[:, e * SEQ + t * P:e * SEQ + (t + 1) * P], slots,
                                                    rt[:, t, 0, e:e + 1], rt[:, t, 6, e:e + 1], ALU.is_equal, ALU.mult)
                    return ins

                pick_tokens([0]).then_inc(me["picks_ready"], 1)
                dve.wait_ge(pair_full, PAIR_AT["gate_row3"] + 2)
                for e in range(NE):
                    for t in range(NT):
                        ins = dve.tensor_scalar(put_raw[:, e // 4, e % 4, t * P:(t + 1) * P], slots,
                                                rt[:, t, 0, e:e + 1], rt[:, t, 7, e:e + 1], ALU.is_equal, ALU.mult)
                ins.then_inc(me["picks_ready"], 1)
                pick_tokens(range(1, NE)).then_inc(me["picks_ready"], 1)

                def next_put(event):
                    dve.tensor_copy(put, put_all[:, bass.ds(event * SEQ, SEQ)]).then_inc(me["put_ready"], 1)

                def add_outputs(event):
                    for i in range(4):
                        t, half = i // 2, i % 2
                        dve.wait_ge(me["put_full"], event * 4 + (i + 1))
                        dst = y_t[:, t, half * W:(half + 1) * W]
                        dve.tensor_tensor(dst, dst, Y_B[2 + i % 2][:], ALU.add).then_inc(me["put_added"], 1)
                    dve.wait_ge(me["put_added"], event * 4 + 4)

                def gathered_low(count, half, buffer):
                    dve.wait_ge(me["ue_hi_ready"], count)
                    flat = [l[:, buffer, 4 * half:4 * half + 4, :].rearrange("p k s -> p (k s)") for l in (ue_hi, ue_lo)]
                    dve.tensor_tensor(flat[1], temp_flat[:, half * W:(half + 1) * W], flat[0].bitcast(F32),
                                      ALU.subtract).then_inc(me["ue_split"], 1)

                for half in range(2):
                    gathered_low(half + 1, half, 0)
                splits.start_pass(p)

                def pair_of_experts(pr, final):
                    splits.start_pair(p, pr, final)
                    for r in range(2):
                        for g in range(EGROUPS):
                            step = r * EGROUPS + g
                            done = pr * (2 * EGROUPS) + step
                            if g >= 1:
                                splits.ahead_in_pair(r, ("gate", g))
                                turned_low(done, W, me["hf_hi_ready"], me["hf_ready"])
                            splits.ahead_in_pair(r, ("up", g))
                            dve.wait_ge(me["silu_ready"], done + 1)
                            dve.wait_ge(me["up_full"], done + 1)
                            h = h_t[:, step % 2, :]
                            dve.tensor_tensor(h, h, UP_B[:], ALU.mult).then_inc(me["h_ready"], 1)
                            if g in (2, 4):
                                half = g // 2 - 1
                                splits.ahead_in_pair(r, ("down", g - 1))
                                gathered_low(pr * 4 + (2 * r + 2 + half + 1), half, (r + 1) % 2)
                            if g == 3:
                                next_put(pr * 2 + r)
                        splits.ahead_in_pair(r, ("down", EGROUPS - 2))
                        turned_low(pr * (2 * EGROUPS) + (r + 1) * EGROUPS, W, me["hf_hi_ready"], me["hf_ready"])
                        add_outputs(pr * 2 + r)
                    splits.ahead_in_pair(1, ("down", EGROUPS - 1), SPLITS)

                with dve.Fori(0, NE // 2 - 1) as pr:
                    pair_of_experts(pr, False)
                pair_of_experts(NE // 2 - 1, True)
                next_put(NE)
                add_outputs(NE)

            experts(0)
            overflow = dve.value_load(flag[0:1, 0:1], min_val=0, max_val=1)
            with dve.If(overflow > 0):
                experts(1)
            norm(3)


_INS = ["x", "c", "positions", "ada_w", "ada_b", "ln_g", "ln_b", "attn_w_in", "attn_w_out", "rec_w_in",
        "rec_lb_logits", "rec_norm_w", "rec_w_out", "ffn_w_gate", "ffn_w_up", "ffn_w_down", "router_w",
        "moe_w_gate", "moe_w_up", "moe_w_down"]


def kernel(**inputs):
    import concourse.bacc as bacc
    from concourse.bass_utils import run_bass_kernel_spmd

    nc = bacc.Bacc("TRN2", target_bir_lowering=False, num_devices=1)
    arrays, args = {}, []
    for name in _INS:
        a = np.ascontiguousarray(inputs[name])
        arrays[f"in_{name}"] = a
        args.append(nc.dram_tensor(f"in_{name}", a.shape, mybir.dt.from_np(a.dtype), kind="ExternalInput").ap())
    out = nc.dram_tensor("out", (1, SEQ, D), F32, kind="ExternalOutput").ap()
    trunk_kernel(nc, *args, out)
    r = run_bass_kernel_spmd(nc, [arrays], core_ids=[0])
    return r.results[0]["out"]
```
